# Optimizing a Trainium2 kernel written in Bass

```python
import jax, jax.numpy as jnp
from jax import lax
import numpy as np

D_MODEL = 1024
BATCH = 1
SEQ = 256
DEPTH = 1

N_MEM = 256
ML_HEADS = 4
ML_DQK = 128
ML_DV = 256
ML_CHUNK = 64
ML_CONV = 4
FX_HEADS = 8
FX_DH = 128
FX_BLOCK = 128
CA_HEADS = 4
CA_DH = 256
N_EXPERTS = 32
TOP_K = 4
D_FF = D_MODEL
SWIGLU_LIMIT = 7.0
SWIGLU_ALPHA = 1.702
EPS = 1e-5
N_BRANCH = 3

ML_QK_W = ML_HEADS * ML_DQK
ML_V_W = ML_HEADS * ML_DV
FX_W = FX_HEADS * FX_DH
CA_W = CA_HEADS * CA_DH
BRANCH_W = 1024
SPLITS = (ML_QK_W, ML_QK_W, ML_V_W, ML_HEADS, ML_HEADS, ML_V_W,
          FX_W, FX_W, FX_W, FX_HEADS, CA_W, N_BRANCH * D_MODEL)
D_IN_PROJ = 2 * ML_QK_W + 2 * ML_V_W + 2 * ML_HEADS + 3 * FX_W + FX_HEADS + CA_W + N_BRANCH * D_MODEL

kernel_name = "hybrid_mlstm_fox_memxattn_moe"

def rmsnorm(x, g):
    xf = x.astype(jnp.float32)
    y = xf * lax.rsqrt(jnp.mean(xf * xf, axis=-1, keepdims=True) + EPS)
    return (y * g.astype(jnp.float32)).astype(x.dtype)

def causal_dwconv(x, w):
    K, C = w.shape
    return lax.conv_general_dilated(
        x, w[:, None, :].astype(x.dtype), window_strides=(1,), padding=[(K - 1, 0)],
        dimension_numbers=("NWC", "WIO", "NWC"), feature_group_count=C)

def mlstm_chunkwise(q, k, v, i_pre, f_pre):
    B, S, H, dqk = q.shape
    dv = v.shape[-1]
    L = ML_CHUNK
    NC = S // L
    f32 = jnp.float32
    q = q.astype(f32) * (dqk ** -0.5)

    def chunks(a):
        return a.astype(f32).reshape(B, NC, L, H, a.shape[-1]).transpose(1, 0, 3, 2, 4)

    def gchunks(a):
        return a.astype(f32).reshape(B, NC, L, H).transpose(1, 0, 3, 2)

    qc, kc, vc = chunks(q), chunks(k), chunks(v)
    ic = gchunks(i_pre)
    lfc = gchunks(jax.nn.log_sigmoid(f_pre.astype(f32)))
    causal = jnp.tril(jnp.ones((L, L), dtype=bool))

    def step(carry, inp):
        C, n, m = carry
        qb, kb, vb, ib, lfb = inp
        b = jnp.cumsum(lfb, axis=-1)
        Dm = jnp.where(causal, b[..., :, None] - b[..., None, :] + ib[..., None, :], -jnp.inf)
        m_inter = b + m[..., None]
        m_t = jnp.maximum(Dm.max(-1), m_inter)
        w_intra = jnp.exp(Dm - m_t[..., None])
        w_inter = jnp.exp(m_inter - m_t)
        s = jnp.einsum("bhtd,bhsd->bhts", qb, kb) * w_intra
        num = jnp.einsum("bhts,bhsv->bhtv", s, vb) + w_inter[..., None] * jnp.einsum("bhtd,bhdv->bhtv", qb, C)
        den = s.sum(-1) + w_inter * jnp.einsum("bhtd,bhd->bht", qb, n)
        h = num / jnp.maximum(jnp.abs(den), jnp.exp(-m_t))[..., None]
        m_new = m_t[..., -1]
        wk = jnp.exp(b[..., -1:] - b + ib - m_new[..., None])
        decay = jnp.exp(b[..., -1] + m - m_new)
        C_new = decay[..., None, None] * C + jnp.einsum("bhsd,bhsv->bhdv", kb * wk[..., None], vb)
        n_new = decay[..., None] * n + jnp.einsum("bhs,bhsd->bhd", wk, kb)
        return (C_new, n_new, m_new), h

    init = (jnp.zeros((B, H, dqk, dv), f32), jnp.zeros((B, H, dqk), f32), jnp.zeros((B, H), f32))
    _, hs = lax.scan(step, init, (qc, kc, vc, ic, lfc))
    return hs.transpose(1, 0, 3, 2, 4).reshape(B, S, H, dv)

def forgetting_attention(q, k, v, f_pre):
    B, S, H, d = q.shape
    NB = S // FX_BLOCK
    f32 = jnp.float32
    c = jnp.cumsum(jax.nn.log_sigmoid(f_pre.astype(f32)), axis=1).transpose(0, 2, 1)
    kh = k.transpose(0, 2, 1, 3)
    vh = v.transpose(0, 2, 1, 3)
    qb = q.reshape(B, NB, FX_BLOCK, H, d).transpose(1, 0, 3, 2, 4)
    cqb = c.reshape(B, H, NB, FX_BLOCK).transpose(2, 0, 1, 3)
    starts = jnp.arange(NB, dtype=jnp.int32) * FX_BLOCK
    kpos = jnp.arange(S, dtype=jnp.int32)
    scale = d ** -0.5

    def block(args):
        qblk, cq, start = args
        s = jnp.einsum("bhqd,bhkd->bhqk", qblk, kh).astype(f32) * scale + cq[..., None] - c[:, :, None, :]
        qpos = start + jnp.arange(FX_BLOCK, dtype=jnp.int32)
        s = jnp.where(kpos[None, :] <= qpos[:, None], s, -jnp.inf)
        p = jax.nn.softmax(s, axis=-1).astype(vh.dtype)
        return jnp.einsum("bhqk,bhkd->bhqd", p, vh)

    out = lax.map(block, (qb, cqb, starts))
    return out.transpose(1, 0, 3, 2, 4).reshape(B, S, H, d)

def memory_attention(q, km, vm):
    s = jnp.einsum("bshd,bmhd->bhsm", q, km).astype(jnp.float32) * (q.shape[-1] ** -0.5)
    p = jax.nn.softmax(s, axis=-1).astype(vm.dtype)
    return jnp.einsum("bhsm,bmhd->bshd", p, vm)

def moe_ffn(h, w_router, b_router, w_exp_in, b_exp_in, w_exp_out, b_exp_out):
    B, S, D = h.shape
    t = h.reshape(B * S, D)
    logits = (t @ w_router + b_router).astype(jnp.float32)
    top_v, top_i = lax.top_k(logits, TOP_K)
    top_w = jax.nn.softmax(top_v, axis=-1)
    combine = jnp.sum(jax.nn.one_hot(top_i, N_EXPERTS, dtype=jnp.float32) * top_w[..., None], axis=1)

    def expert_step(acc, p):
        w1, b1, w2, b2, ce = p
        u = t @ w1 + b1
        g = jnp.minimum(u[:, :D_FF], SWIGLU_LIMIT)
        lin = jnp.clip(u[:, D_FF:], -SWIGLU_LIMIT, SWIGLU_LIMIT)
        a = g * jax.nn.sigmoid(SWIGLU_ALPHA * g) * (lin + 1)
        y = a @ w2 + b2
        return acc + ce[:, None].astype(y.dtype) * y, None

    out, _ = lax.scan(expert_step, jnp.zeros_like(t), (w_exp_in, b_exp_in, w_exp_out, b_exp_out, combine.T))
    return out.reshape(B, S, D)

def setup_inputs(seed: int = 0) -> dict:
    key = jax.random.key(seed)
    ks = jax.random.split(key, 24)
    f32 = jnp.float32
    nrm = lambda k, shape, s: jax.random.normal(k, shape, f32) * s
    Ld = DEPTH
    return {
        "x": nrm(ks[0], (BATCH, SEQ, D_MODEL), 1.0),
        "mem": nrm(ks[1], (BATCH, N_MEM, D_MODEL), 1.0),
        "norm_mix": 1.0 + nrm(ks[2], (Ld, D_MODEL), 0.1),
        "w_in": nrm(ks[3], (Ld, D_MODEL, D_IN_PROJ), D_MODEL ** -0.5),
        "b_ml_gates": jnp.concatenate([nrm(ks[4], (Ld, ML_HEADS), 0.1),
                                       3.0 + nrm(ks[5], (Ld, ML_HEADS), 0.5)], axis=-1),
        "conv_ml": nrm(ks[6], (Ld, ML_CONV, 2 * ML_QK_W), ML_CONV ** -0.5),
        "ml_head_norm": 1.0 + nrm(ks[7], (Ld, ML_V_W), 0.1),
        "b_fx_gate": 1.0 + nrm(ks[8], (Ld, FX_HEADS), 0.5),
        "norm_mem": 1.0 + nrm(ks[9], (Ld, D_MODEL), 0.1),
        "w_mem_kv": nrm(ks[10], (Ld, D_MODEL, 2 * CA_W), D_MODEL ** -0.5),
        "w_branch": nrm(ks[11], (Ld, N_BRANCH, BRANCH_W, D_MODEL), BRANCH_W ** -0.5),
        "w_out": nrm(ks[12], (Ld, D_MODEL, D_MODEL), D_MODEL ** -0.5),
        "norm_moe": 1.0 + nrm(ks[13], (Ld, D_MODEL), 0.1),
        "w_router": nrm(ks[14], (Ld, D_MODEL, N_EXPERTS), D_MODEL ** -0.5),
        "b_router": nrm(ks[15], (Ld, N_EXPERTS), 0.01),
        "w_exp_in": nrm(ks[16], (Ld, N_EXPERTS, D_MODEL, 2 * D_FF), D_MODEL ** -0.5),
        "b_exp_in": nrm(ks[17], (Ld, N_EXPERTS, 2 * D_FF), 0.01),
        "w_exp_out": nrm(ks[18], (Ld, N_EXPERTS, D_FF, D_MODEL), D_FF ** -0.5),
        "b_exp_out": nrm(ks[19], (Ld, N_EXPERTS, D_MODEL), 0.01),
        "norm_final": 1.0 + nrm(ks[20], (D_MODEL,), 0.1),
    }

def reference(x, mem, norm_mix, w_in, b_ml_gates, conv_ml, ml_head_norm, b_fx_gate, norm_mem,
              w_mem_kv, w_branch, w_out, norm_moe, w_router, b_router, w_exp_in, b_exp_in,
              w_exp_out, b_exp_out, norm_final):
    B, S, D = x.shape
    M = mem.shape[1]
    offsets = np.cumsum(SPLITS)[:-1].tolist()
    for l in range(DEPTH):
        h = rmsnorm(x, norm_mix[l])
        proj = h @ w_in[l]
        (ml_q, ml_k, ml_v, ml_i, ml_f, ml_o, fx_q, fx_k, fx_v, fx_f, ca_q, gates) = jnp.split(proj, offsets, axis=-1)

        qk = jax.nn.silu(causal_dwconv(jnp.concatenate([ml_q, ml_k], axis=-1), conv_ml[l]))
        mq = qk[..., :ML_QK_W].reshape(B, S, ML_HEADS, ML_DQK)
        mk = qk[..., ML_QK_W:].reshape(B, S, ML_HEADS, ML_DQK)
        mv = ml_v.reshape(B, S, ML_HEADS, ML_DV)
        hm = mlstm_chunkwise(mq, mk, mv, ml_i + b_ml_gates[l, :ML_HEADS], ml_f + b_ml_gates[l, ML_HEADS:])
        hm = hm * lax.rsqrt(jnp.mean(hm * hm, axis=-1, keepdims=True) + EPS)
        hm = hm.reshape(B, S, ML_V_W) * ml_head_norm[l].astype(jnp.float32)
        y_ml = (hm * jax.nn.sigmoid(ml_o.astype(jnp.float32))).astype(x.dtype)

        y_fx = forgetting_attention(fx_q.reshape(B, S, FX_HEADS, FX_DH), fx_k.reshape(B, S, FX_HEADS, FX_DH),
                                    fx_v.reshape(B, S, FX_HEADS, FX_DH), fx_f + b_fx_gate[l]).reshape(B, S, FX_W)

        kv = rmsnorm(mem, norm_mem[l]) @ w_mem_kv[l]
        y_ca = memory_attention(ca_q.reshape(B, S, CA_HEADS, CA_DH),
                                kv[..., :CA_W].reshape(B, M, CA_HEADS, CA_DH),
                                kv[..., CA_W:].reshape(B, M, CA_HEADS, CA_DH)).reshape(B, S, CA_W)

        ybr = jnp.stack([y_ml, y_fx, y_ca], axis=2)
        pbr = jnp.einsum("bsnc,ncd->bsnd", ybr, w_branch[l])
        g = jax.nn.sigmoid(gates.reshape(B, S, N_BRANCH, D))
        merged = jnp.sum(g * pbr, axis=2)
        x = x + merged @ w_out[l]

        x = x + moe_ffn(rmsnorm(x, norm_moe[l]), w_router[l], b_router[l], w_exp_in[l], b_exp_in[l],
                        w_exp_out[l], b_exp_out[l])
    return rmsnorm(x, norm_final)


_drawn_inputs = setup_inputs


def setup_inputs(seed=0):
    import zlib

    import numpy as np

    out = dict(_drawn_inputs(seed))
    spreads = {}
    factors = {'b_exp_in': 8.0, 'b_exp_out': 8.0}
    for name, (base, spread) in spreads.items():
        noise = np.random.default_rng([zlib.crc32(name.encode()), seed]).standard_normal(out[name].shape)
        drawn = base * np.exp(spread * noise) if base else spread * noise
        out[name] = __import__('jax').numpy.asarray(drawn.astype(out[name].dtype))
    for name, factor in factors.items():
        out[name] = (out[name] * factor).astype(out[name].dtype)
    return out
```

```python
import concourse.bass as bass
from concourse import mybir
from contextlib import ExitStack

F32 = mybir.dt.float32
I32 = mybir.dt.int32
U32 = mybir.dt.uint32
ALU = mybir.AluOpType
ACT = mybir.ActivationFunctionType
AX = mybir.AxisListType

P = 128
D = 1024
KT = D // P
S = 256
TT = S // P
ML_H, ML_DV = 4, 256
FX_H, CA_H = 8, 4
NE, TOPK, FF = 32, 4, 1024
EPS = 1e-5
LIMIT, ALPHA = 7.0, 1.702
FX_SCALE = float(128) ** -0.5
ML_SCALE = float(128) ** -0.5
CA_SCALE = float(256) ** -0.5
UW = 512
RING = 6
UPE = 6
CAP = 64
PUT_BANKS = (7, 4, 5, 2)
ROUNDS = S // CAP

C_QK, C_V, C_I, C_F, C_O = 0, 1024, 2048, 2052, 2056
C_FQ, C_FK, C_FV, C_FF, C_CQ, C_G = 3080, 4104, 5128, 6152, 6160, 7184

SEGMENTS = [("mlqk", "T"), ("mlv", "N"), ("mlo", "N"), ("fxq", "T"), ("fxk", "T"), ("fxv", "N"),
            ("mk", "T"), ("mv", "N"), ("caq", "T"), ("g0", "T"), ("b0", "T"), ("g1", "T"),
            ("b1", "T"), ("g2", "T"), ("b2", "T"), ("out", "N")]
UNITS = [(name, kind, j) for name, kind in SEGMENTS for j in range(2)]
SLOTS = [(name, kind, j, half) for name, kind, j in UNITS for half in range(2)]
ON_DVE = {"b0", "b1", "b2", "out"}
FIRST = {name: 4 * i for i, (name, _) in enumerate(SEGMENTS)}

STAGES = {}


def _stage(slot, *work):
    STAGES.setdefault(slot, []).append(work)


for _i in range(4):
    _stage(_i, "conv", _i)
_stage(1, "gates")
_stage(5, "gate_columns")
_stage(6, "mem_turn")
for _h in range(ML_H):
    _stage(8 + _h, "ml_scores", _h)
    _stage(9 + _h, "ml_values", _h)
_stage(13, "ml_norm")
_stage(14, "ml_turn")
for _h in range(FX_H):
    _stage(24 + _h, "fx_scores", _h)
    _stage(25 + _h, "fx_turn", _h)
    _stage(26 + _h, "fx_values", _h)
for _h in range(CA_H):
    _stage(36 + _h, "ca_scores", _h)
    _stage(37 + _h, "ca_turn", _h)
    _stage(38 + _h, "ca_values", _h)

BANK_USERS = {
    4: [("x", 0), ("gates", 0), ("mem", 0)] + [("ml_s", h) for h in range(4)] + [("ml_y", 0)]
       + [("fx_s", h) for h in range(8)] + [("ca_s", h) for h in range(4)] + [("moe", 0)],
    5: [("x", 1), ("gcol", 0), ("mem", 1)] + [("ml_m", h) for h in range(4)] + [("ml_y", 1)]
       + [("fx_p", h) for h in range(8)] + [("ca_p", h) for h in range(4)] + [("moe", 1)],
    6: [("x", 2), ("mem", 2)] + [("ml_n0", h) for h in range(4)] + [("ml_y", 2)]
       + [("fx_o", h) for h in range(8)] + [("ca_o", h) for h in range(4)] + [("moe", 2)],
    7: [("rows", 0), ("x", 3), ("mem", 3)] + [("ml_n1", h) for h in range(4)] + [("ml_y", 3), ("moe", 3)],
}


def turn(bank, user):
    return BANK_USERS[bank].index(user) + 1


def act_drains(i):
    return sum(SLOTS[n][0] not in ON_DVE for n in range(i + 1))


def dve_drains(i):
    return sum(SLOTS[n][0] in ON_DVE for n in range(i + 1))


def build(nc, x, mem, norm_mix, w_in, b_ml_gates, conv_ml, ml_head_norm, b_fx_gate, norm_mem,
          w_mem_kv, w_branch, w_out, norm_moe, w_router, b_router, w_exp_in, b_exp_in,
          w_exp_out, b_exp_out, norm_final, out):
    ctx = ExitStack()
    with ctx:
        def sb(name, shape, dt=F32):
            return ctx.enter_context(nc.sbuf_tensor(name, shape, dt))

        def sem(name):
            return ctx.enter_context(nc.semaphore(name))

        ring = [sb(f"ring{b}", [P, KT, UW]) for b in range(RING)]
        bank = [ctx.enter_context(nc.psum_tensor(f"bank{b}", [P, 512], F32)) for b in range(8)]

        xs = sb("xs", [P, TT, D])
        hT = sb("hT", [P, KT, S])
        big_a = sb("big_a", [P, 2 * (D + 4)])
        xn = big_a[:, 0:2 * D].rearrange("p (t d) -> p t d", t=TT)
        num = big_a[:, :].rearrange("p (t h v) -> p t h v", t=TT, h=ML_H)
        gsig = big_a[:, 0:2 * D].rearrange("p (c s) -> p c s", c=KT)
        big_b = sb("big_b", [P, 2 * D])
        memT = big_b[:, :].rearrange("p (c s) -> p c s", c=KT)
        caqT = memT
        gfin = big_b[:, D:2 * D]
        b2rows = big_b[0:NE, 0:D]
        merged = sb("merged", [P, KT, S])
        qkT, kmT = merged, merged
        big_c = sb("big_c", [P, KT * (S + 3)])
        pre = big_c[:, :].rearrange("p (c s) -> p c s", c=KT)
        ymlT = big_c[:, 0:KT * S].rearrange("p (c s) -> p c s", c=KT)
        b1rows = big_c[:, 0:2 * FF]
        square_dump = [big_a[:, D * t:D * (t + 1)] for t in range(TT)]
        big_e = sb("big_e", [P, TT * ML_H * (ML_DV + 1)])
        mval = big_e[:, :].rearrange("p (t h v) -> p t h v", t=TT, h=ML_H)
        vm = big_e[:, 0:2 * D].rearrange("p (t d) -> p t d", t=TT)
        big_f = sb("big_f", [P, 2 * D])
        sig_o = big_f[:, :].rearrange("p (t d) -> p t d", t=TT)
        ycaT = big_f[:, :].rearrange("p (c s) -> p c s", c=KT)
        fxqT = sb("fxqT", [P, KT, S])
        yfxT = fxqT
        fxkT = sb("fxkT", [P, KT, S])
        fxv = sb("fxv", [P, TT, D])
        mems = fxv

        ident = sb("ident", [P, P])
        before = sb("before", [P, P])
        ones = sb("ones", [P, P])
        fxmask = sb("fxmask", [P, 384])
        pick = sb("pick", [12, 12, P])
        slots_f = sb("slots_f", [P, CAP * ROUNDS + CAP])
        eps = sb("eps", [P, 1])
        rows = sb("rows", [64, P])
        cols = sb("cols", [P, 64])
        g_mix, g_mem, g_moe, g_head = (cols[:, 8 * i:8 * i + 8] for i in range(4))
        conv_c = cols[:, 32:64].rearrange("p (j c) -> p j c", j=4)
        wg = sb("wg", [P, KT, 16])
        bF = sb("bF", [12, 1])
        bI = sb("bI", [4, 1])
        wr = sb("wr", [P, KT, NE])
        br = sb("br", [P, NE])
        ss = sb("ss", [P, 2, 4])
        std = sb("std", [P, 2, 4])
        rstd = sb("rstd", [P, 2, 4])
        fpre, fabs, fexp, fln, lf, grow = (big_b[0:12, S * n:S * (n + 1)] for n in range(6))
        ipre = grow[0:4, :]
        cF = sb("cF", [12, S])
        arow = sb("arow", [4, S])
        mrun = sb("mrun", [4, S])
        mrow = sb("mrow", [4, S])
        acol = sb("acol", [P, TT, 4])
        floor = sb("floor", [P, TT, 4])
        p_a = sb("p_a", [P, 512])
        p_b = sb("p_b", [P, 512])
        p_t = sb("p_t", [P, 512])
        negmax = sb("negmax", [P, 2])
        esum = sb("esum", [P, 2])
        rsum = sb("rsum", [P, 2])
        den = sb("den", [P, TT, 4])
        rden = sb("rden", [P, TT, 4])
        fac = sb("fac", [P, TT, 4])
        msq = sb("msq", [P, TT, 4])

        tn = fxv
        tT = hT
        moe_a = fxqT[:, :, :].rearrange("p c s -> p (c s)")
        moe_b = fxkT[:, :, :].rearrange("p c s -> p (c s)")
        got = moe_a[:, 0:512]
        gotT = moe_a[:, 512:1024].rearrange("p (q h c) -> p q h c", q=4, h=2)
        aT = moe_a[:, 1024:1536].rearrange("p (q h c) -> p q h c", q=4, h=2)
        selWT = moe_a[:, 1536:1792].rearrange("p (t n) -> p t n", t=TT)
        gate, lin, sig, act_out = (moe_b[:, 512 * n:512 * (n + 1)] for n in range(4))
        yS = big_e[:, 0:512]
        pick_e = sb("pick_e", [P, CAP])
        sel = sb("sel", [P, TT, CAP])
        selW = sb("selW", [P, TT, 2, CAP])
        logits = sb("logits", [P, TT, NE])
        top = sb("top", [P, TT, 8])
        topi = sb("topi", [P, TT, 8], U32)
        topf = sb("topf", [P, TT, 8])
        topw = sb("topw", [P, TT, TOPK])
        hot = sb("hot", [P, TT, TOPK, NE])
        mask = sb("mask", [P, TT, NE])
        comb = sb("comb", [P, TT, NE + 2])
        rank = sb("rank", [P, TT, NE + 2])
        combT = sb("combT", [NE, S])
        most = sb("most", [P, 1], I32)

        weights_in = [sem(f"weights_in{b}") for b in range(RING)]
        weights_used = [sem(f"expert_unit{j}_used") for j in range(UPE)]
        x_in, mem_in, rows_in, gatew_in, gateb_in = (sem(n) for n in ("x_in", "mem_in", "rows_in", "gatew_in", "gateb_in"))
        router_in, b1_in, b2_in, final_in, out_sent = (sem(n) for n in ("router_in", "b1_in", "b2_in", "final_in", "out_sent"))
        consts = sem("consts")
        pool_step = sem("pool_step")
        proj_done = sem("proj_done")
        act_drained, dve_drained = sem("act_drained"), sem("dve_drained")
        filled = {b: sem(f"bank{b}_filled") for b in range(4, 8)}
        drained = {b: sem(f"bank{b}_drained") for b in range(4, 8)}
        squares = sem("squares")
        std_ready = sem("std_ready")
        scaled = sem("scaled")
        cols_ready = sem("cols_ready")
        hT_ready = sem("hT_ready")
        memT_ready = sem("memT_ready")
        ml_ready = sem("ml_ready")
        pre_zero = sem("pre_zero")
        conv_sum, conv_sig, qk_ready = sem("conv_sum"), sem("conv_sig"), sem("qk_ready")
        gate_lin, gate_log, gates_ready = sem("gate_lin"), sem("gate_log"), sem("gates_ready")
        act_step = sem("act_step")
        col_ready = sem("col_ready")
        ml_arg, ml_exp, ml_masked = sem("ml_arg"), sem("ml_exp"), sem("ml_masked")
        ml_num, ml_ms, ml_std, ml_y = sem("ml_num"), sem("ml_ms"), sem("ml_std"), sem("ml_y")
        ymlT_ready = sem("ymlT_ready")
        max_ready, exp_ready, prob_ready, pt_ready, y_ready = (sem(n) for n in ("max_ready", "exp_ready", "prob_ready", "pt_ready", "y_ready"))
        dve_step = sem("dve_step")
        tT_ready, logits_done, topm_ready, topw_exp = (sem(n) for n in ("tT_ready", "logits_done", "topm_ready", "topw_exp"))
        mask_ready, rank_done, route_ready, comb_turned, combT_ready = (sem(n) for n in ("mask_ready", "rank_done", "route_ready", "comb_turned", "combT_ready"))
        bias_done = sem("bias_done")
        sel_ready, selW_ready, gather_done, got_ready = (sem(n) for n in ("sel_ready", "selW_ready", "gather_done", "got_ready"))
        got_turned, gotT_ready, pick_ready, act_turned, act_ready = (sem(n) for n in ("got_turned", "gotT_ready", "pick_ready", "act_turned", "act_ready"))
        b1_zero = sem("b1_zero")
        selT_done, selWT_ready = sem("selT_done"), sem("selWT_ready")
        gate_ready, sig_ready, ffn_step, aT_ready = (sem(n) for n in ("gate_ready", "sig_ready", "ffn_step", "aT_ready"))
        yS_ready, put_done, put_added = (sem(n) for n in ("yS_ready", "put_done", "put_added"))
        moe_end, final_std, final_sq, final_ready = (sem(n) for n in ("moe_end", "final_std", "final_sq", "final_ready"))

        block = ctx.enter_context(nc.Block())

        def unit_source(name, j):
            base = {"mlqk": C_QK, "mlv": C_V, "mlo": C_O, "fxq": C_FQ, "fxk": C_FK, "fxv": C_FV,
                    "caq": C_CQ, "g0": C_G, "g1": C_G + D, "g2": C_G + 2 * D}
            if name in base:
                m, c = w_in[0], base[name]
            elif name in ("mk", "mv"):
                m, c = w_mem_kv[0], D * (name == "mv")
            elif name == "out":
                m, c = w_out[0], 0
            else:
                m, c = w_branch[0, int(name[1])], 0
            return m[:, c + UW * j:c + UW * (j + 1)].rearrange("(k p) n -> p k n", p=P)

        def expert_slot(j):
            b = (len(UNITS) + j) % RING
            return b, len(range(b, len(UNITS), RING))

        def for_rounds(eng, body):
            eng.wait_ge(route_ready, 1)
            busiest = eng.value_load(most[0:1, 0:1], min_val=0, max_val=S)
            with eng.Fori(0, ROUNDS) as r:
                with eng.If(busiest > r * CAP):
                    body(r)

        @block.sync
        def _(sp):
            sp.dma_start(xs[:, :, :], x[0].rearrange("(t p) d -> p t d", p=P)).then_inc(x_in, 16)
            for u, (name, kind, j) in enumerate(UNITS):
                b = u % RING
                if u >= RING:
                    sp.wait_ge(proj_done, 2 * (u - RING) + 2)
                sp.dma_start(ring[b][:, :, :], unit_source(name, j)).then_inc(weights_in[b], 16)
                if u == 1:
                    sp.dma_start(mems[:, :, :], mem[0].rearrange("(t p) d -> p t d", p=P)).then_inc(mem_in, 16)

            def load_unit(e, j):
                b, _ = expert_slot(j)
                w = w_exp_in if j < 4 else w_exp_out
                c = UW * (j if j < 4 else j - 4)
                src = w[0, e:e + 1, :, c:c + UW] if isinstance(e, int) else w[0, bass.ds(e, 1), :, c:c + UW]
                sp.dma_start(ring[b][:, :, :], src.rearrange("e (k p) n -> p (e k) n", p=P)).then_inc(weights_in[b], 16)

            def load_expert(n, e):
                for j in range(UPE):
                    sp.wait_ge(weights_used[j], n)
                    load_unit(e, j)

            for j in range(UPE):
                sp.wait_ge(proj_done, 2 * (len(UNITS) - RING + j) + 2)
                load_unit(0, j)
            with sp.Fori(1, NE) as e:
                load_expert(e, e)
            sp.wait_ge(route_ready, 1)
            busiest = sp.value_load(most[0:1, 0:1], min_val=0, max_val=S)
            with sp.Fori(1, ROUNDS) as r:
                with sp.If(busiest > r * CAP):
                    with sp.Fori(0, NE) as e:
                        load_expert(r * NE + e, e)
            for t in range(TT):
                sp.wait_ge(final_ready, t + 1)
                sp.dma_start(out[0].rearrange("(t p) d -> p t d", p=P)[:, t, :], tn[:, t, :]).then_inc(out_sent, 16)
            sp.wait_ge(out_sent, 16 * TT)

        @block.gpsimd
        def _(pool):
            pool.memset(ident[:, :], 0.0).then_inc(pool_step, 1)
            pool.memset(before[:, :], 1.0).then_inc(pool_step, 1)
            pool.memset(fxmask[:, :], 0.0).then_inc(pool_step, 1)
            pool.memset(pick[:, :, :], 0.0).then_inc(pool_step, 1)
            pool.memset(ones[:, :], 1.0).then_inc(consts, 1)
            pool.memset(eps[:, :], EPS).then_inc(consts, 1)
            pool.memset(mval[:, :, :, ML_DV:ML_DV + 1], 1.0).then_inc(consts, 1)
            pool.wait_ge(pool_step, 4)
            pool.affine_select(out=ident[:, :], in_=ident[:, :], compare_op=ALU.not_equal, fill=1.0,
                               base=0, pattern=[[-1, P]], channel_multiplier=1).then_inc(consts, 1)
            pool.affine_select(out=before[:, :], in_=before[:, :], compare_op=ALU.is_gt, fill=0.0,
                               base=0, pattern=[[1, P]], channel_multiplier=-1).then_inc(consts, 1)
            pool.affine_select(out=pick[:, :, :], in_=pick[:, :, :], compare_op=ALU.not_equal, fill=-1.0,
                               base=0, pattern=[[-1, 12], [0, P]], channel_multiplier=1).then_inc(consts, 1)
            for c in (0, 256):
                pool.affine_select(out=fxmask[:, c:c + P], in_=fxmask[:, c:c + P], compare_op=ALU.is_ge,
                                   fill=-1e30, base=0, pattern=[[-1, P]], channel_multiplier=1).then_inc(consts, 1)
            pool.iota(slots_f[:, :], [[1, CAP * (ROUNDS + 1)]], base=0, channel_multiplier=0,
                      allow_small_or_imprecise_dtypes=True).then_inc(consts, 1)
            for h in range(ML_H):
                pool.wait_ge(ml_exp, h + 1)
                for n, c in enumerate((0, 256)):
                    pool.affine_select(out=p_b[:, c:c + P], in_=p_b[:, c:c + P], compare_op=ALU.is_ge,
                                       fill=0.0, base=0, pattern=[[1, P]],
                                       channel_multiplier=-1).then_inc(ml_masked, 1)
            pool.wait_ge(proj_done, 45)
            pool.memset(b1rows, 0.0).then_inc(b1_zero, 1)

        ALL_CONSTS = 9

        @block.scalar
        def _(act):
            act.dma_start(rows[0:8, :], norm_mix[0].rearrange("(r n) -> r n", n=P)).then_inc(rows_in, 16)
            act.dma_start(rows[8:16, :], norm_mem[0].rearrange("(r n) -> r n", n=P)).then_inc(rows_in, 16)
            act.dma_start(rows[16:24, :], norm_moe[0].rearrange("(r n) -> r n", n=P)).then_inc(rows_in, 16)
            act.dma_start(rows[24:32, :], ml_head_norm[0].rearrange("(r n) -> r n", n=P)).then_inc(rows_in, 16)
            act.dma_start(rows[32:64, :], conv_ml[0].rearrange("j (r n) -> (j r) n", n=P)).then_inc(rows_in, 16)
            wv = w_in[0].rearrange("(k p) n -> p k n", p=P)
            act.dma_start(wg[:, :, 0:4], wv[:, :, C_F:C_F + 4]).then_inc(gatew_in, 16)
            act.dma_start(wg[:, :, 4:12], wv[:, :, C_FF:C_FF + 8]).then_inc(gatew_in, 16)
            act.dma_start(wg[:, :, 12:16], wv[:, :, C_I:C_I + 4]).then_inc(gatew_in, 16)
            act.dma_start(bI[:, :], b_ml_gates[0, 0:4].rearrange("(a n) -> a n", n=1)).then_inc(gateb_in, 16)
            act.dma_start(bF[0:4, :], b_ml_gates[0, 4:8].rearrange("(a n) -> a n", n=1)).then_inc(gateb_in, 16)
            act.dma_start(bF[4:12, :], b_fx_gate[0].rearrange("(a n) -> a n", n=1)).then_inc(gateb_in, 16)

            def square_sums(src, n):
                for t in range(TT):
                    ins = act.activation(p_scratch[t], src[:, t, :], ACT.Square, accum_out=ss[:, t, 0:1])
                    ins.then_inc(squares, 1)
                act.wait_ge(squares, 2 * n + 2)
                act.activation(std[:, :, 0:1], ss[:, :, 0:1], ACT.Sqrt, bias=eps[:, 0:1],
                               scale=1.0 / D).then_inc(std_ready, 1)

            p_scratch = [fxkT[:, 4 * t:4 * t + 4, :].rearrange("p c s -> p (c s)") for t in range(TT)]
            act.wait_ge(x_in, 16)
            act.wait_ge(consts, ALL_CONSTS)
            square_sums(xs, 0)
            act.wait_ge(mem_in, 16)
            act.wait_ge(scaled, 2)
            square_sums(mems, 1)

            def drain(i):
                name, kind, j, half = SLOTS[i]
                if name in ON_DVE:
                    return
                act.wait_ge(proj_done, i + 1)
                src = bank[i % 4][:, :]
                pair = src.rearrange("p (c s) -> p c s", c=2)
                c0 = 4 * j + 2 * half
                fun, scale = ACT.Copy, 1.0
                if name == "mlqk":
                    dst, src = pre[:, c0:c0 + 2, 3:S + 3], pair
                elif name == "mlv":
                    dst = mval[:, half, 2 * j:2 * j + 2, 0:ML_DV]
                    src = src.rearrange("p (h v) -> p h v", h=2)
                elif name == "mlo":
                    dst, fun = sig_o[:, half, UW * j:UW * (j + 1)], ACT.Sigmoid
                elif name == "fxq":
                    dst, src, scale = fxqT[:, c0:c0 + 2, :], pair, FX_SCALE
                elif name == "fxk":
                    dst, src = fxkT[:, c0:c0 + 2, :], pair
                elif name == "fxv":
                    dst = fxv[:, half, UW * j:UW * (j + 1)]
                elif name == "mk":
                    dst, src = kmT[:, c0:c0 + 2, :], pair
                elif name == "mv":
                    dst = vm[:, half, UW * j:UW * (j + 1)]
                elif name == "caq":
                    dst, src = caqT[:, c0:c0 + 2, :], pair
                else:
                    if name in ("g1", "g2"):
                        act.wait_ge(dve_drained, 4 * int(name[1]))
                    dst, src, fun = gsig[:, c0:c0 + 2, :], pair, ACT.Sigmoid
                act.activation(dst, src, fun, scale=scale).then_inc(act_drained, 1)

            def conv(i):
                act.wait_ge(conv_sum, 8 * (i + 1))
                act.activation(p_b[:, :], p_a[:, :], ACT.Sigmoid).then_inc(conv_sig, 1)

            def gates():
                act.wait_ge(gate_lin, 1)
                act.activation(fabs, fpre, ACT.Abs).then_inc(act_step, 1)
                act.wait_ge(act_step, 1)
                act.activation(fexp, fabs, ACT.Exp, scale=-1.0).then_inc(act_step, 1)
                act.wait_ge(act_step, 2)
                act.activation(fln, fexp, ACT.Ln, bias=1.0).then_inc(gate_log, 1)

            def gate_columns():
                act.wait_ge(filled[5], turn(5, ("gcol", 0)))
                col = bank[5][:, 0:16].rearrange("p (w t h) -> p w t h", w=2, t=TT)
                act.activation(acol[:, :, :], col[:, 0], ACT.Copy)
                act.activation(floor[:, :, :], col[:, 1], ACT.Exp, scale=-1.0).then_inc(drained[5], 1)

            def ml_scores(h):
                act.wait_ge(ml_arg, h + 1)
                act.wait_ge(drained[5], turn(5, ("ml_m", h)))
                if h:
                    act.wait_ge(drained[4], turn(4, ("ml_s", h - 1)))
                act.activation(p_b[:, 0:384], p_a[:, 0:384], ACT.Exp).then_inc(ml_exp, 1)

            def ml_values(h):
                for t in range(TT):
                    act.wait_ge(filled[6 + t], turn(6 + t, (f"ml_n{t}", h)))
                    act.activation(p_scr[ML_H * t + h], bank[6 + t][:, 0:ML_DV], ACT.Square,
                                   accum_out=ss[:, t, h:h + 1]).then_inc(ml_num, 1)
                    act.activation(num[:, t, h, :], bank[6 + t][:, 0:ML_DV + 1],
                                   ACT.Copy).then_inc(drained[6 + t], 1)

            p_scr = [fxv[:, t, ML_DV * h:ML_DV * (h + 1)] for t in range(TT) for h in range(ML_H)]

            def ml_norm():
                act.wait_ge(ml_ms, 1)
                act.activation(std[:, :, :], msq[:, :, :], ACT.Sqrt, bias=eps[:, 0:1],
                               scale=1.0 / ML_DV).then_inc(ml_std, 1)

            def fx_scores(h):
                act.wait_ge(max_ready, h + 1)
                if h:
                    act.wait_ge(filled[5], turn(5, ("fx_p", h - 1)))
                act.activation(p_b[:, 0:128], p_a[:, 0:128], ACT.Exp, bias=negmax[:, 0:1],
                               accum_out=esum[:, 0:1]).then_inc(exp_ready, 1)
                act.activation(p_b[:, 128:384], p_a[:, 128:384], ACT.Exp, bias=negmax[:, 1:2],
                               accum_out=esum[:, 1:2]).then_inc(exp_ready, 1)

            def fx_turn(h):
                act.wait_ge(filled[5], turn(5, ("fx_p", h)))
                if h:
                    act.wait_ge(filled[6], turn(6, ("fx_o", h - 1)))
                act.activation(p_t[:, 0:384], bank[5][:, 0:384], ACT.Copy).then_inc(drained[5], 1)

            def fx_values(h):
                act.wait_ge(filled[6], turn(6, ("fx_o", h)))
                act.activation(yfxT[:, h, :], bank[6][:, 0:S], ACT.Copy).then_inc(drained[6], 1)

            def ca_scores(h):
                act.wait_ge(max_ready, FX_H + h + 1)
                if h:
                    act.wait_ge(filled[5], turn(5, ("ca_p", h - 1)))
                for t in range(TT):
                    ins = act.activation(p_b[:, S * t:S * (t + 1)], bank[4][:, S * t:S * (t + 1)], ACT.Exp,
                                         bias=negmax[:, t:t + 1], scale=CA_SCALE, accum_out=esum[:, t:t + 1])
                    ins.then_inc(drained[4] if t else exp_ready, 1)

            def ca_turn(h):
                act.wait_ge(filled[5], turn(5, ("ca_p", h)))
                if h:
                    act.wait_ge(filled[6], turn(6, ("ca_o", h - 1)))
                act.activation(p_t[:, :], bank[5][:, :], ACT.Copy).then_inc(drained[5], 1)

            def ca_values(h):
                act.wait_ge(filled[6], turn(6, ("ca_o", h)))
                act.activation(ycaT[:, 2 * h:2 * h + 2, :], bank[6][:, :].rearrange("p (c s) -> p c s", c=2),
                               ACT.Copy).then_inc(drained[6], 1)

            work = dict(conv=conv, gates=gates, gate_columns=gate_columns, ml_scores=ml_scores,
                        ml_values=ml_values, ml_norm=ml_norm, fx_scores=fx_scores, fx_turn=fx_turn,
                        fx_values=fx_values, ca_scores=ca_scores, ca_turn=ca_turn,
                        ca_values=ca_values)
            for i in range(len(SLOTS)):
                drain(i)
                for name, *arg in STAGES.get(i, []):
                    if name in work:
                        work[name](*arg)
                if i == 0:
                    act.dma_start(wr[:, :, :], w_router[0].rearrange("(k p) e -> p k e", p=P)).then_inc(router_in, 16)
                    act.dma_start(br[:, :], b_router[0].partition_broadcast(P)).then_inc(router_in, 16)
                if i == 44:
                    act.wait_ge(proj_done, 45)
                    act.dma_start(gfin, norm_final.partition_broadcast(P)).then_inc(final_in, 16)
                    act.dma_start(b2rows, b_exp_out[0]).then_inc(b2_in, 16)
                    act.wait_ge(b1_zero, 1)
                    act.dma_start(b1rows[0:NE, :], b_exp_in[0]).then_inc(b1_in, 16)

            p_scratch = square_dump
            act.wait_ge(dve_drained, dve_drains(len(SLOTS) - 1))
            square_sums(xs, 2)
            act.wait_ge(topm_ready, 1)
            for t in range(TT):
                act.activation(topw[:, t, :], top[:, t, 0:TOPK], ACT.Exp, bias=negmax[:, t:t + 1],
                               accum_out=esum[:, t:t + 1]).then_inc(topw_exp, 1)
            act.wait_ge(comb_turned, 1)
            act.activation(combT[:, :], bank[1][0:NE, 0:S], ACT.Copy).then_inc(combT_ready, 1)

            def keep_gathered(k):
                act.wait_ge(gather_done, k)
                act.activation(got, bank[2][:, :], ACT.Copy).then_inc(got_ready, 1)

            def experts(r):
                keep_gathered(r * (NE + 1) + 1)
                with act.Fori(0, NE) as e:
                    n = r * NE + e
                    act.wait_ge(gate_ready, n + 1)
                    act.activation(sig, gate, ACT.Sigmoid, scale=ALPHA).then_inc(sig_ready, 1)
                    keep_gathered(n + r + 2)
                    act.wait_ge(selT_done, n + 1)
                    act.activation(selWT, bank[6][:, 0:S].rearrange("p (t n) -> p t n", t=TT),
                                   ACT.Copy).then_inc(selWT_ready, 1)
                    act.wait_ge(act_turned, n + 1)
                    act.activation(aT, bank[4][:, :].rearrange("p (q h c) -> p q h c", q=4, h=2),
                                   ACT.Copy).then_inc(aT_ready, 1)
                    act.wait_ge(weights_used[5], n + 1)
                    act.activation(yS, bank[5][:, :], ACT.Copy).then_inc(yS_ready, 1)

            for_rounds(act, experts)
            act.wait_ge(moe_end, 1)
            for t in range(TT):
                act.activation(square_dump[t], xs[:, t, :], ACT.Square, accum_out=ss[:, t, 0:1]).then_inc(final_sq, 1)
            act.wait_ge(final_sq, 2)
            act.activation(std[:, :, 0:1], ss[:, :, 0:1], ACT.Sqrt, bias=eps[:, 0:1], scale=1.0 / D).then_inc(final_std, 1)

        @block.vector
        def _(dve):
            steps = [0]

            def step(ins):
                steps[0] += 1
                ins.then_inc(dve_step, 1)
                dve.wait_ge(dve_step, steps[0])

            def scale_rows(src, dst, n):
                dve.wait_ge(std_ready, n + 1)
                step(dve.reciprocal(rstd[:, :, 0:1], std[:, :, 0:1]))
                for t in range(TT):
                    dve.tensor_scalar(dst[:, t, :], src[:, t, :], rstd[:, t, 0:1], None, ALU.mult).then_inc(scaled, 1)

            def drain_turned(dst, user, g, done):
                for q in range(4):
                    dve.wait_ge(filled[4 + q], turn(4 + q, (user, q)))
                    for c in range(2):
                        ins = dve.tensor_scalar(dst[:, 2 * q + c, :], bank[4 + q][:, S * c:S * (c + 1)],
                                                g[:, 2 * q + c:2 * q + c + 1], None, ALU.mult)
                        if c == 0:
                            ins.then_inc(done, 1)
                        else:
                            ins.then_inc(drained[4 + q], 1)

            dve.memset(pre[:, :, 0:3], 0.0).then_inc(pre_zero, 1)
            scale_rows(xs, xn, 0)
            dve.wait_ge(filled[7], turn(7, ("rows", 0)))
            dve.tensor_copy(cols[:, :], bank[7][:, 0:64]).then_inc(drained[7], 1)
            dve.wait_ge(drained[7], 1)
            drain_turned(hT, "x", g_mix, hT_ready)

            def drain(i):
                name, kind, j, half = SLOTS[i]
                if name not in ON_DVE:
                    return
                dve.wait_ge(proj_done, i + 1)
                if name == "out":
                    cut = slice(UW * j, UW * (j + 1))
                    dve.tensor_tensor(xs[:, half, cut], bank[i % 4][:, :], xs[:, half, cut], ALU.add).then_inc(dve_drained, 1)
                    return
                c0 = 4 * j + 2 * half
                pair = bank[i % 4][:, :].rearrange("p (c s) -> p c s", c=2)
                if c0 == 0:
                    dve.wait_ge(act_drained, act_drains(i))
                if name == "b0":
                    dve.tensor_tensor(merged[:, c0:c0 + 2, :], pair, gsig[:, c0:c0 + 2, :], ALU.mult).then_inc(dve_drained, 1)
                    return
                step(dve.tensor_tensor(gsig[:, c0:c0 + 2, :], pair, gsig[:, c0:c0 + 2, :], ALU.mult))
                dve.tensor_tensor(merged[:, c0:c0 + 2, :], merged[:, c0:c0 + 2, :], gsig[:, c0:c0 + 2, :],
                                  ALU.add).then_inc(dve_drained, 1)

            def conv(i):
                dve.wait_ge(act_drained, i + 1)
                if i == 0:
                    dve.wait_ge(pre_zero, 1)
                else:
                    dve.wait_ge(qk_ready, i)
                for tap in range(4):
                    for c in range(2):
                        a = p_a[:, S * c:S * (c + 1)]
                        src = pre[:, 2 * i + c, tap:tap + S]
                        w = conv_c[:, tap, 2 * i + c:2 * i + c + 1]
                        if tap == 0:
                            ins = dve.tensor_scalar(a, src, w, None, ALU.mult)
                        else:
                            ins = dve.scalar_tensor_tensor(out=a, in0=src, scalar=w, in1=a, op0=ALU.mult, op1=ALU.add)
                        ins.then_inc(conv_sum, 1)
                    dve.wait_ge(conv_sum, 8 * i + 2 * tap + 2)
                dve.wait_ge(conv_sig, i + 1)
                dve.tensor_tensor(qkT[:, 2 * i:2 * i + 2, :], p_a[:, :].rearrange("p (c s) -> p c s", c=2),
                                  p_b[:, :].rearrange("p (c s) -> p c s", c=2), ALU.mult).then_inc(qk_ready, 1)

            def gates():
                dve.wait_ge(gateb_in, 48)
                dve.wait_ge(filled[4], turn(4, ("gates", 0)))
                step(dve.tensor_scalar(ipre, bank[4][0:4, S:2 * S], bI[:, 0:1], None, ALU.add))
                dve.tensor_scalar(fpre, bank[4][0:12, 0:S], bF[:, 0:1], None, ALU.add).then_inc(gate_lin, 1)
                dve.wait_ge(gate_lin, 1)
                dve.wait_ge(gate_log, 1)
                step(dve.scalar_tensor_tensor(out=lf, in0=fpre, scalar=0.0, in1=fln,
                                              op0=ALU.min, op1=ALU.subtract))
                dve.wait_ge(consts, ALL_CONSTS)
                step(dve.memset(fabs, 1.0))
                step(dve.tensor_tensor_scan(cF[:, :], fabs, lf, 0.0, ALU.mult, ALU.add))
                step(dve.tensor_tensor(arow[:, :], ipre, cF[0:4, :], ALU.subtract))
                step(dve.tensor_tensor_scan(mrun[:, :], arow[:, :], arow[:, :], 0.0, ALU.max, ALU.max))
                dve.tensor_tensor(mrow[:, :], mrun[:, :], cF[0:4, :], ALU.add).then_inc(drained[4], 1)

            def mem_turn():
                drain_turned(memT, "mem", g_mem, memT_ready)

            def ml_scores(h):
                dve.wait_ge(filled[5], turn(5, ("ml_m", h)))
                if h == 0:
                    dve.wait_ge(drained[5], turn(5, ("gcol", 0)))
                dve.tensor_scalar(p_a[:, 0:256], bank[5][:, 0:256], acol[:, 0, h:h + 1], 0.0,
                                  ALU.add, ALU.min).then_inc(ml_arg, 1)
                dve.tensor_scalar(p_a[:, 256:384], bank[5][:, 256:384], acol[:, 1, h:h + 1], 0.0,
                                  ALU.add, ALU.min).then_inc(drained[5], 1)
                dve.wait_ge(ml_masked, 2 * h + 2)
                dve.wait_ge(filled[4], turn(4, ("ml_s", h)))
                if h:
                    dve.wait_ge(filled[7], turn(7, ("ml_n1", h - 1)))
                dve.scalar_tensor_tensor(out=p_t[:, 0:384], in0=bank[4][:, 0:384], scalar=ML_SCALE,
                                         in1=p_b[:, 0:384], op0=ALU.mult, op1=ALU.mult).then_inc(drained[4], 1)

            def ml_norm():
                dve.wait_ge(drained[6], turn(6, ("ml_n0", 3)))
                dve.wait_ge(drained[7], turn(7, ("ml_n1", 3)))
                dve.wait_ge(ml_num, 8)
                step(dve.tensor_scalar(den[:, :, :], num[:, :, :, ML_DV:ML_DV + 1].rearrange("p t h o -> p t (h o)"),
                                       -1.0, None, ALU.mult))
                step(dve.tensor_tensor(den[:, :, :], num[:, :, :, ML_DV:ML_DV + 1].rearrange("p t h o -> p t (h o)"),
                                       den[:, :, :], ALU.max))
                step(dve.tensor_tensor(den[:, :, :], den[:, :, :], floor[:, :, :], ALU.max))
                step(dve.reciprocal(rden[:, :, :], den[:, :, :]))
                step(dve.tensor_tensor(msq[:, :, :], ss[:, :, :], rden[:, :, :], ALU.mult))
                dve.tensor_tensor(msq[:, :, :], msq[:, :, :], rden[:, :, :], ALU.mult).then_inc(ml_ms, 1)
                dve.wait_ge(ml_std, 1)
                step(dve.reciprocal(fac[:, :, :], std[:, :, :]))
                step(dve.tensor_tensor(fac[:, :, :], fac[:, :, :], rden[:, :, :], ALU.mult))
                dve.wait_ge(act_drained, act_drains(FIRST["mlo"] + 3))
                for t in range(TT):
                    for h in range(ML_H):
                        v = num[:, t, h, 0:ML_DV]
                        dve.scalar_tensor_tensor(out=v, in0=v, scalar=fac[:, t, h:h + 1],
                                                 in1=sig_o[:, t, ML_DV * h:ML_DV * (h + 1)],
                                                 op0=ALU.mult, op1=ALU.mult).then_inc(ml_y, 1)

            def ml_turn():
                drain_turned(ymlT, "ml_y", g_head, ymlT_ready)

            def normalise(cuts):
                step(dve.reciprocal(rsum[:, :], esum[:, :]))
                for t, (a, b) in enumerate(cuts):
                    dve.tensor_scalar(p_b[:, a:b], p_b[:, a:b], rsum[:, t:t + 1], None, ALU.mult).then_inc(prob_ready, 1)

            def fx_scores(h):
                dve.wait_ge(filled[4], turn(4, ("fx_s", h)))
                dve.tensor_tensor(p_a[:, 0:384], bank[4][:, 0:384], fxmask[:, :], ALU.add).then_inc(drained[4], 1)
                dve.wait_ge(drained[4], turn(4, ("fx_s", h)))
                step(dve.tensor_reduce(negmax[:, 0:1], p_a[:, 0:128], AX.X, ALU.max, negate=True))
                dve.tensor_reduce(negmax[:, 1:2], p_a[:, 128:384], AX.X, ALU.max, negate=True).then_inc(max_ready, 1)
                dve.wait_ge(exp_ready, 2 * h + 2)
                normalise(((0, 128), (128, 384)))

            def ca_scores(h):
                dve.wait_ge(filled[4], turn(4, ("ca_s", h)))
                step(dve.tensor_reduce(negmax[:, :], bank[4][:, :].rearrange("p (t m) -> p t m", t=TT), AX.X, ALU.max))
                dve.tensor_scalar(negmax[:, :], negmax[:, :], -CA_SCALE, None, ALU.mult).then_inc(max_ready, 1)
                dve.wait_ge(exp_ready, 2 * FX_H + h + 1)
                dve.wait_ge(drained[4], turn(4, ("ca_s", h)))
                normalise(((0, 256), (256, 512)))

            work = dict(conv=conv, gates=gates, mem_turn=mem_turn, ml_scores=ml_scores, ml_norm=ml_norm,
                        ml_turn=ml_turn, fx_scores=fx_scores, ca_scores=ca_scores)
            for i in range(len(SLOTS)):
                drain(i)
                for name, *arg in STAGES.get(i, []):
                    if name in work:
                        work[name](*arg)
                if i == 4:
                    scale_rows(mems, xn, 1)

            dve.wait_ge(dve_drained, dve_drains(len(SLOTS) - 1))
            scale_rows(xs, tn, 2)
            drain_turned(tT, "moe", g_moe, tT_ready)
            dve.wait_ge(router_in, 32)
            dve.wait_ge(logits_done, 1)
            for t in range(TT):
                step(dve.tensor_tensor(logits[:, t, :], bank[0][:, NE * t:NE * (t + 1)], br[:, :], ALU.add))
                step(dve.max(top[:, t, :], logits[:, t, :]))
                step(dve.max_index(topi[:, t, :], top[:, t, :], logits[:, t, :]))
            step(dve.tensor_copy(topf[:, :, :], topi[:, :, :]))
            dve.tensor_scalar(negmax[:, :], top[:, :, 0:1].rearrange("p t o -> p (t o)"), -1.0, None,
                              ALU.mult).then_inc(topm_ready, 1)
            experts_iota = slots_f[:, 0:NE].unsqueeze(1).unsqueeze(1).to_broadcast([P, TT, TOPK, NE])
            step(dve.tensor_tensor(hot[:, 0], slots_f[:, 0:NE].unsqueeze(1).to_broadcast([P, TOPK, NE]),
                                   topf[:, 0, 0:TOPK].unsqueeze(2).to_broadcast([P, TOPK, NE]), ALU.is_equal))
            step(dve.tensor_tensor(hot[:, 1], slots_f[:, 0:NE].unsqueeze(1).to_broadcast([P, TOPK, NE]),
                                   topf[:, 1, 0:TOPK].unsqueeze(2).to_broadcast([P, TOPK, NE]), ALU.is_equal))
            dve.tensor_reduce(mask[:, :, :], hot[:, :, :, :].rearrange("p t j e -> p t e j"), AX.X,
                              ALU.add).then_inc(mask_ready, 1)
            dve.memset(comb[:, :, NE:NE + 2], 0.0)
            step(dve.memset(rank[:, :, NE:NE + 2], -1.0))
            dve.wait_ge(topw_exp, 2)
            step(dve.reciprocal(rsum[:, :], esum[:, :]))
            dve.wait_ge(mask_ready, 1)
            for t in range(TT):
                step(dve.tensor_scalar(topw[:, t, :], topw[:, t, :], rsum[:, t:t + 1], None, ALU.mult))
                step(dve.tensor_tensor(hot[:, t], hot[:, t], topw[:, t, :].unsqueeze(2).to_broadcast([P, TOPK, NE]),
                                       ALU.mult))
            step(dve.tensor_reduce(comb[:, :, 0:NE], hot[:, :, :, :].rearrange("p t j e -> p t e j"), AX.X, ALU.add))
            dve.wait_ge(rank_done, 1)
            counts = bank[0][:, 128:192].rearrange("p (t e) -> p t e", t=TT)
            step(dve.scalar_tensor_tensor(out=rank[:, :, 0:NE], in0=counts, scalar=1.0, in1=mask[:, :, :],
                                          op0=ALU.add, op1=ALU.mult))
            step(dve.tensor_scalar(rank[:, :, 0:NE], rank[:, :, 0:NE], 1.0, None, ALU.subtract))
            dve.tensor_reduce(most[:, :], bank[0][:, 192:224], AX.X, ALU.max).then_inc(route_ready, 1)

            for q in range(4):
                t, c = q // 2, q % 2
                dve.wait_ge(bias_done, q + 1)
                cut = slice(512 * c, 512 * (c + 1))
                dve.tensor_tensor(xs[:, t, cut], bank[4 + q][:, :], xs[:, t, cut], ALU.add).then_inc(put_added, 1)
            dve.wait_ge(put_added, 4)

            def select(r, e):
                for t in range(TT):
                    ins = dve.tensor_scalar(sel[:, t, :], slots_f[:, bass.ds(r * CAP, CAP)], rank[:, t, bass.ds(e, 1)],
                                            None, ALU.is_equal)
                    ins.then_inc(sel_ready, 1)

            def select_weighted(r, e):
                for t in range(TT):
                    twice = slots_f[:, bass.ds(r * CAP, CAP)].unsqueeze(1).to_broadcast([P, 2, CAP])
                    ins = dve.tensor_scalar(selW[:, t, :, :], twice, rank[:, t, bass.ds(e, 1)],
                                            comb[:, t, bass.ds(e, 1)], ALU.is_equal, ALU.mult)
                    ins.then_inc(selW_ready, 1)

            def pick_expert(e):
                dve.tensor_copy(pick_e[:, :], ident[:, bass.ds(e, 1)].to_broadcast([P, CAP])).then_inc(pick_ready, 1)

            def take_turned(k):
                dve.wait_ge(got_turned, k)
                weights = g_moe.rearrange("p (h q) -> p q h", h=2)
                for h in range(2):
                    dve.tensor_tensor(gotT[:, :, h, :],
                                      bank[3][:, :].rearrange("p (q h c) -> p q h c", q=4, h=2)[:, :, h, :],
                                      weights[:, :, h].unsqueeze(2).to_broadcast([P, 4, CAP]),
                                      ALU.mult).then_inc(gotT_ready, 1)

            def experts(r):
                select(r, 0)
                select_weighted(r, 0)
                pick_expert(0)
                dve.wait_ge(gather_done, r * (NE + 1) + 1)
                select(r, 1)
                take_turned(r * (NE + 1) + 1)
                with dve.Fori(0, NE) as e:
                    n = r * NE + e
                    dve.wait_ge(weights_used[1], n + 1)
                    dve.tensor_scalar(gate, bank[0][:, :], LIMIT, None, ALU.min).then_inc(gate_ready, 1)
                    dve.wait_ge(weights_used[3], n + 1)
                    dve.tensor_scalar(lin, bank[1][:, :], LIMIT, -LIMIT, ALU.min, ALU.max).then_inc(ffn_step, 1)
                    dve.wait_ge(gate_ready, n + 1)
                    dve.wait_ge(ffn_step, n * 2 + 1)
                    dve.scalar_tensor_tensor(out=lin, in0=lin, scalar=1.0, in1=gate, op0=ALU.add,
                                             op1=ALU.mult).then_inc(ffn_step, 1)
                    dve.wait_ge(ffn_step, n * 2 + 2)
                    dve.wait_ge(sig_ready, n + 1)
                    dve.tensor_tensor(act_out, lin, sig, ALU.mult).then_inc(act_ready, 1)
                    pick_expert(e + 1)
                    dve.wait_ge(gather_done, n + r + 2)
                    select(r, e + 2)
                    dve.wait_ge(selT_done, n + 1)
                    select_weighted(r, e + 1)
                    take_turned(n + r + 2)
                    for q, b in enumerate(PUT_BANKS):
                        t, half = q // 2, q % 2
                        dst = xs[:, t, 512 * half:512 * (half + 1)]
                        dve.wait_ge(put_done, n * 4 + q + 1)
                        dve.tensor_tensor(dst, bank[b][:, :], dst, ALU.add).then_inc(put_added, 1)

            for_rounds(dve, experts)
            dve.memset(negmax[:, :], 0.0).then_inc(moe_end, 1)
            dve.wait_ge(final_std, 1)
            step(dve.reciprocal(rstd[:, :, 0:1], std[:, :, 0:1]))
            dve.wait_ge(final_in, 16)
            for t in range(TT):
                dve.scalar_tensor_tensor(out=tn[:, t, :], in0=xs[:, t, :], scalar=rstd[:, t, 0:1], in1=gfin,
                                         op0=ALU.mult, op1=ALU.mult).then_inc(final_ready, 1)

        @block.tensor
        def _(pe):
            mm = pe.matmul

            def claim(b, user):
                if turn(b, user) > 1:
                    pe.wait_ge(drained[b], turn(b, user) - 1)

            def turn_rows(src, user):
                for q in range(4):
                    claim(4 + q, (user, q))
                    for c in range(2):
                        for t in range(TT):
                            ins = pe.transpose(bank[4 + q][:, S * c + P * t:S * c + P * (t + 1)],
                                               src(t, 2 * q + c), ident[:, :])
                    ins.then_inc(filled[4 + q], 1)

            pe.wait_ge(consts, ALL_CONSTS)
            pe.wait_ge(rows_in, 80)
            pe.transpose(bank[7][:, 0:64], rows[:, :], ident[0:64, 0:64]).then_inc(filled[7], 1)
            pe.wait_ge(scaled, 2)
            turn_rows(lambda t, c: xn[:, t, P * c:P * (c + 1)], "x")
            for q in range(4):
                pe.wait_ge(drained[4 + q], turn(4 + q, ("x", q)))

            rhs_of = {"b0": ymlT, "b1": yfxT, "b2": ycaT, "mk": memT, "mv": memT, "out": merged}

            def project(i):
                name, kind, j, half = SLOTS[i]
                u = i // 2
                w = ring[u % RING]
                if half == 0:
                    pe.wait_ge(weights_in[u % RING], 16 * (u // RING + 1))
                if i >= 4:
                    if SLOTS[i - 4][0] in ON_DVE:
                        pe.wait_ge(dve_drained, dve_drains(i - 4))
                    else:
                        pe.wait_ge(act_drained, act_drains(i - 4))
                if j == 0 and half == 0:
                    if name in ("mk", "mv"):
                        pe.wait_ge(memT_ready, 4)
                        for q in range(4):
                            pe.wait_ge(drained[4 + q], turn(4 + q, ("mem", q)))
                    elif name == "b0":
                        pe.wait_ge(ymlT_ready, 4)
                        for q in range(4):
                            pe.wait_ge(drained[4 + q], turn(4 + q, ("ml_y", q)))
                    elif name == "b1":
                        pe.wait_ge(drained[6], turn(6, ("fx_o", FX_H - 1)))
                    elif name == "b2":
                        pe.wait_ge(drained[6], turn(6, ("ca_o", CA_H - 1)))
                    elif name == "out":
                        pe.wait_ge(dve_drained, dve_drains(i - 1))
                act_in = rhs_of.get(name, hT)
                o = bank[i % 4]
                if kind == "T":
                    for c in range(2):
                        col = P * (2 * half + c)
                        for k in range(KT):
                            ins = mm(o[:, S * c:S * (c + 1)], w[:, k, col:col + P], act_in[:, k, :],
                                     start=(k == 0), stop=(k == KT - 1))
                else:
                    for k in range(KT):
                        ins = mm(o[:, :], act_in[:, k, P * half:P * (half + 1)], w[:, k, :],
                                 start=(k == 0), stop=(k == KT - 1))
                ins.then_inc(proj_done, 1)

            def gates():
                pe.wait_ge(gatew_in, 48)
                claim(4, ("gates", 0))
                for k in range(KT):
                    mm(bank[4][0:12, 0:S], wg[:, k, 0:12], hT[:, k, :], start=(k == 0), stop=(k == KT - 1))
                for k in range(KT):
                    ins = mm(bank[4][0:4, S:2 * S], wg[:, k, 12:16], hT[:, k, :], start=(k == 0), stop=(k == KT - 1))
                ins.then_inc(filled[4], 1)

            def gate_columns():
                pe.wait_ge(drained[4], turn(4, ("gates", 0)))
                claim(5, ("gcol", 0))
                for w, row in enumerate((arow, mrow)):
                    for t in range(TT):
                        c = 8 * w + 4 * t
                        ins = pe.transpose(bank[5][:, c:c + 4], row[:, P * t:P * (t + 1)], ident[0:4, 0:4])
                ins.then_inc(filled[5], 1)

            def mem_turn():
                pe.wait_ge(scaled, 4)
                turn_rows(lambda t, c: xn[:, t, P * c:P * (c + 1)], "mem")

            def ml_scores(h):
                if h == 0:
                    pe.wait_ge(qk_ready, 4)
                claim(5, ("ml_m", h))
                mm(bank[5][:, 0:256], pick[0:4, h, :], mrun[:, :], start=True, stop=True)
                mm(bank[5][:, 256:384], pick[0:4, h, :], mrun[:, P:S], start=True, stop=True).then_inc(filled[5], 1)
                claim(4, ("ml_s", h))
                mm(bank[4][:, 0:256], qkT[:, ML_H + h, 0:P], qkT[:, h, :], start=True, stop=True)
                mm(bank[4][:, 256:384], qkT[:, ML_H + h, P:S], qkT[:, h, P:S], start=True, stop=True).then_inc(filled[4], 1)

            def ml_values(h):
                pe.wait_ge(drained[4], turn(4, ("ml_s", h)))
                if h == 0:
                    pe.wait_ge(act_drained, act_drains(FIRST["mlv"] + 3))
                claim(6, ("ml_n0", h))
                mm(bank[6][:, 0:ML_DV + 1], p_t[:, 0:P], mval[:, 0, h, :], start=True, stop=True).then_inc(filled[6], 1)
                claim(7, ("ml_n1", h))
                mm(bank[7][:, 0:ML_DV + 1], p_t[:, P:S], mval[:, 0, h, :], start=True, stop=False)
                mm(bank[7][:, 0:ML_DV + 1], p_t[:, S:384], mval[:, 1, h, :], start=False, stop=True).then_inc(filled[7], 1)

            def ml_turn():
                pe.wait_ge(ml_y, 8)
                turn_rows(lambda t, c: num[:, t, c // 2, P * (c % 2):P * (c % 2 + 1)], "ml_y")

            def fx_scores(h):
                if h == 0:
                    pe.wait_ge(act_drained, act_drains(FIRST["fxk"] + 3))
                claim(4, ("fx_s", h))
                mm(bank[4][:, 0:128], fxqT[:, h, 0:P], fxkT[:, h, 0:P], start=True, stop=False)
                mm(bank[4][:, 0:128], pick[:, 4 + h, :], cF[:, 0:P], start=False, stop=True)
                mm(bank[4][:, 128:384], fxqT[:, h, P:S], fxkT[:, h, :], start=True, stop=False)
                mm(bank[4][:, 128:384], pick[:, 4 + h, :], cF[:, :], start=False, stop=True).then_inc(filled[4], 1)

            def fx_turn(h):
                pe.wait_ge(prob_ready, 2 * h + 2)
                claim(5, ("fx_p", h))
                for q in range(3):
                    ins = pe.transpose(bank[5][:, P * q:P * (q + 1)], p_b[:, P * q:P * (q + 1)], ident[:, :])
                ins.then_inc(filled[5], 1)

            def fx_values(h):
                pe.wait_ge(drained[5], turn(5, ("fx_p", h)))
                if h == 0:
                    pe.wait_ge(act_drained, act_drains(FIRST["fxv"] + 3))
                claim(6, ("fx_o", h))
                mm(bank[6][:, 0:S], fxv[:, 0, P * h:P * (h + 1)], p_t[:, 0:S], start=True, stop=False)
                mm(bank[6][:, P:S], fxv[:, 1, P * h:P * (h + 1)], p_t[:, S:384], start=False, stop=True).then_inc(filled[6], 1)

            def ca_scores(h):
                if h == 0:
                    pe.wait_ge(act_drained, act_drains(FIRST["caq"] + 3))
                claim(4, ("ca_s", h))
                for t in range(TT):
                    for k in range(2):
                        ins = mm(bank[4][:, S * t:S * (t + 1)], caqT[:, 2 * h + k, P * t:P * (t + 1)],
                                 kmT[:, 2 * h + k, :], start=(k == 0), stop=(k == 1))
                ins.then_inc(filled[4], 1)

            def ca_turn(h):
                pe.wait_ge(prob_ready, 2 * (FX_H + h) + 2)
                claim(5, ("ca_p", h))
                for m in range(2):
                    for t in range(TT):
                        ins = pe.transpose(bank[5][:, S * m + P * t:S * m + P * (t + 1)],
                                           p_b[:, S * t + P * m:S * t + P * (m + 1)], ident[:, :])
                ins.then_inc(filled[5], 1)

            def ca_values(h):
                pe.wait_ge(drained[5], turn(5, ("ca_p", h)))
                claim(6, ("ca_o", h))
                for c in range(2):
                    for m in range(2):
                        col = 256 * h + P * c
                        ins = mm(bank[6][:, S * c:S * (c + 1)], vm[:, m, col:col + P], p_t[:, S * m:S * (m + 1)],
                                 start=(m == 0), stop=(m == 1))
                ins.then_inc(filled[6], 1)

            work = dict(gates=gates, gate_columns=gate_columns, mem_turn=mem_turn, ml_scores=ml_scores,
                        ml_values=ml_values, ml_turn=ml_turn, fx_scores=fx_scores, fx_turn=fx_turn,
                        fx_values=fx_values, ca_scores=ca_scores, ca_turn=ca_turn, ca_values=ca_values)
            for i in range(len(SLOTS)):
                project(i)
                for name, *arg in STAGES.get(i, []):
                    if name in work:
                        work[name](*arg)

            pe.wait_ge(scaled, 6)
            turn_rows(lambda t, c: tn[:, t, P * c:P * (c + 1)], "moe")
            pe.wait_ge(router_in, 32)
            for q in range(4):
                pe.wait_ge(drained[4 + q], turn(4 + q, ("moe", q)))
            pe.wait_ge(tT_ready, 4)
            pe.wait_ge(dve_drained, dve_drains(len(SLOTS) - 1))
            for t in range(TT):
                for k in range(KT):
                    ins = mm(bank[0][:, NE * t:NE * (t + 1)], tT[:, k, P * t:P * (t + 1)], wr[:, k, :],
                             start=(k == 0), stop=(k == KT - 1))
            ins.then_inc(logits_done, 1)
            pe.wait_ge(mask_ready, 1)
            mm(bank[0][:, 128:160], before[:, :], mask[:, 0, :], start=True, stop=True)
            mm(bank[0][:, 160:192], ones[:, :], mask[:, 0, :], start=True, stop=False)
            mm(bank[0][:, 160:192], before[:, :], mask[:, 1, :], start=False, stop=True)
            mm(bank[0][:, 192:224], ones[:, :], mask[:, 0, :], start=True, stop=False)
            mm(bank[0][:, 192:224], ones[:, :], mask[:, 1, :], start=False, stop=True).then_inc(rank_done, 1)
            pe.wait_ge(route_ready, 1)
            for t in range(TT):
                ins = pe.transpose(bank[1][0:NE, P * t:P * (t + 1)], comb[:, t, 0:NE], ident[:, :])
            ins.then_inc(comb_turned, 1)
            pe.wait_ge(combT_ready, 1)
            pe.wait_ge(b2_in, 16)
            for q in range(4):
                t, c = q // 2, q % 2
                mm(bank[4 + q][:, :], combT[:, P * t:P * (t + 1)], b2rows[:, 512 * c:512 * (c + 1)],
                   start=True, stop=True).then_inc(bias_done, 1)
            pe.wait_ge(put_added, 4)

            def both_halves(o, lhsT, low, high, start, stop):
                mm(o[0:CAP, :], lhsT, low, start=start, stop=stop)
                return mm(o[CAP:P, :], lhsT, high, start=start, stop=stop)

            def gather(k):
                pe.wait_ge(sel_ready, k)
                for t in range(TT):
                    ins = both_halves(bank[2], sel[:, t, :], tn[:, t, 0:512], tn[:, t, 512:D], t == 0, t == TT - 1)
                ins.then_inc(gather_done, 1)

            def turn_gathered(k):
                pe.wait_ge(got_ready, k)
                for q in range(4):
                    ins = pe.transpose(bank[3][:, P * q:P * (q + 1)], got[:, P * q:P * (q + 1)], ident[:, :])
                ins.then_inc(got_turned, 1)

            pe.wait_ge(b1_in, 16)

            def experts(r):
                gather(r * (2 * (NE + 2)) + 2)
                turn_gathered(r * (NE + 1) + 1)
                with pe.Fori(0, NE) as e:
                    n = r * NE + e
                    pe.wait_ge(pick_ready, n + r + 1)
                    pe.wait_ge(gotT_ready, n * 2 + r * 2 + 2)
                    for part in range(2):
                        o, c = bank[part], FF * part
                        both_halves(o, pick_e[:, :], b1rows[:, c:c + 512], b1rows[:, c + 512:c + FF], True, False)
                        pair = [expert_slot(2 * part + j)[0] for j in range(2)]
                        for j, b in enumerate(pair):
                            pe.wait_ge(weights_in[b], n * 16 + 16 * (expert_slot(2 * part + j)[1] + 1))
                        for k in range(KT):
                            x_k = gotT[:, k % 4, k // 4, :]
                            low = mm(o[0:CAP, :], x_k, ring[pair[0]][:, k, :], start=False, stop=(k == KT - 1))
                            high = mm(o[CAP:P, :], x_k, ring[pair[1]][:, k, :], start=False, stop=(k == KT - 1))
                        low.then_inc(weights_used[2 * part], 1)
                        high.then_inc(weights_used[2 * part + 1], 1)
                    pe.wait_ge(selW_ready, n * 2 + r * 2 + 2)
                    pe.wait_ge(put_added, n * 4 + 4)
                    gather(n * 2 + r * 4 + 4)
                    for t in range(TT):
                        ins = pe.transpose(bank[6][:, P * t:P * (t + 1)],
                                           selW[:, t, :, :].rearrange("p o c -> p (o c)"), ident[:, :])
                    ins.then_inc(selT_done, 1)
                    pe.wait_ge(act_ready, n + 1)
                    for q in range(4):
                        ins = pe.transpose(bank[4][:, P * q:P * (q + 1)], act_out[:, P * q:P * (q + 1)], ident[:, :])
                    ins.then_inc(act_turned, 1)
                    pair = [expert_slot(4 + j)[0] for j in range(2)]
                    pe.wait_ge(weights_in[pair[0]], n * 16 + 16 * (expert_slot(4)[1] + 1))
                    pe.wait_ge(weights_in[pair[1]], n * 16 + 16 * (expert_slot(5)[1] + 1))
                    pe.wait_ge(aT_ready, n + 1)
                    for k in range(KT):
                        a_k = aT[:, k % 4, k // 4, :]
                        low = mm(bank[5][0:CAP, :], a_k, ring[pair[0]][:, k, :], start=(k == 0), stop=(k == KT - 1))
                        high = mm(bank[5][CAP:P, :], a_k, ring[pair[1]][:, k, :], start=(k == 0), stop=(k == KT - 1))
                    low.then_inc(weights_used[4], 1)
                    high.then_inc(weights_used[5], 1)
                    turn_gathered(n + r + 2)
                    pe.wait_ge(selWT_ready, n + 1)
                    pe.wait_ge(yS_ready, n + 1)
                    for q, b in enumerate(PUT_BANKS):
                        t, half = q // 2, slice(CAP * (q % 2), CAP * (q % 2 + 1))
                        mm(bank[b][:, :], selWT[half, t, :], yS[half, :], start=True, stop=True).then_inc(put_done, 1)

            for_rounds(pe, experts)


_INS = ["x", "mem", "norm_mix", "w_in", "b_ml_gates", "conv_ml", "ml_head_norm", "b_fx_gate", "norm_mem",
        "w_mem_kv", "w_branch", "w_out", "norm_moe", "w_router", "b_router", "w_exp_in", "b_exp_in",
        "w_exp_out", "b_exp_out", "norm_final"]


def kernel(**inputs):
    import numpy as np
    import concourse.bacc as bacc
    from concourse.bass_utils import run_bass_kernel_spmd

    nc = bacc.Bacc("TRN2", target_bir_lowering=False, num_devices=1, dynamic_dma_scratch_size=1024)
    arrays, args = {}, []
    for name in _INS:
        a = np.ascontiguousarray(inputs[name])
        arrays[f"in_{name}"] = a
        args.append(nc.dram_tensor(f"in_{name}", a.shape, mybir.dt.from_np(a.dtype), kind="ExternalInput").ap())
    args.append(nc.dram_tensor("out_x", (1, S, D), F32, kind="ExternalOutput").ap())
    build(nc, *args)
    r = run_bass_kernel_spmd(nc, [arrays], core_ids=[0])
    return r.results[0]["out_x"]
```

```python
import concourse.bass as bass
from concourse import mybir
from contextlib import ExitStack

F32 = mybir.dt.float32
F32R = mybir.dt.float32r
I32 = mybir.dt.int32
U32 = mybir.dt.uint32
ALU = mybir.AluOpType
ACT = mybir.ActivationFunctionType
AX = mybir.AxisListType

P = 128
D = 1024
KT = D // P
S = 256
TT = S // P
ML_H, ML_DV = 4, 256
FX_H, CA_H = 8, 4
NE, TOPK, FF = 32, 4, 1024
EPS = 1e-5
LIMIT, ALPHA = 7.0, 1.702
FX_SCALE = float(128) ** -0.5
ML_SCALE = float(128) ** -0.5
CA_SCALE = float(256) ** -0.5
UW = 512
HW = UW // 2
RING = 3
W1, W2 = 2 * FF // UW, D // UW
AHEAD = 9
CAP = 64
PUT_BANKS = (7, 4, 5, 2)
ROUNDS = S // CAP

C_QK, C_V, C_I, C_F, C_O = 0, 1024, 2048, 2052, 2056
C_FQ, C_FK, C_FV, C_FF, C_CQ, C_G = 3080, 4104, 5128, 6152, 6160, 7184

SEGMENTS = [("mlqk", "T"), ("mlv", "N"), ("mlo", "N"), ("fxq", "T"), ("fxk", "T"), ("fxv", "N"),
            ("mk", "T"), ("mv", "N"), ("caq", "T"), ("g0", "T"), ("b0", "T"), ("g1", "T"),
            ("b1", "T"), ("g2", "T"), ("b2", "T"), ("out", "N")]
UNITS = [(name, kind, j) for name, kind in SEGMENTS for j in range(2)]
SLOTS = [(name, kind, j, half) for name, kind, j in UNITS for half in range(2)]
ON_DVE = {"b0", "b1", "b2", "out"}
FIRST = {name: 4 * i for i, (name, _) in enumerate(SEGMENTS)}

LAST_B2 = FIRST["b2"] + 3

STAGES = {}


def _stage(slot, *work):
    STAGES.setdefault(slot, []).append(work)


for _i in range(4):
    _stage(2 * _i, "conv", _i)
    _stage(2 * _i + 1, "conv_silu", _i)
_stage(1, "gate_tokens")
_stage(3, "gates")
_stage(4, "gate_logs")
_stage(5, "gate_sums")
_stage(6, "gate_columns")
_stage(7, "mem_turn")
for _h in range(ML_H):
    _stage(8 + _h, "ml_scores", _h)
    _stage(9 + _h, "ml_values", _h)
_stage(13, "ml_norm")
_stage(34, "ml_turn")
_stage(45, "split_fx")
_stage(53, "split_ca")
for _q in range(3):
    _stage(61 + _q, "turn_out", _q)
for _h in range(FX_H):
    _stage(24 + _h, "fx_scores", _h)
    _stage(25 + _h, "fx_turn", _h)
    _stage(26 + _h, "fx_values", _h)
for _h in range(CA_H):
    _stage(36 + _h, "ca_scores", _h)
    _stage(37 + _h, "ca_turn", _h)
    _stage(38 + _h, "ca_values", _h)

BANK_USERS = {
    4: [("x", 0), ("gtok", 0), ("gates", 0), ("mem", 0)] + [("ml_s", h) for h in range(4)]
       + [("fx_s", h) for h in range(8)] + [("ml_y", 0)] + [("ca_s", h) for h in range(4)]
       + [("moe", 0), ("moe", 3)],
    5: [("x", 1), ("gcol", 0), ("mem", 1)] + [("ml_m", h) for h in range(4)]
       + [("fx_p", h) for h in range(8)] + [("ml_y", 1)] + [("ca_p", h) for h in range(4)]
       + [("moe", 1)],
    6: [("x", 2), ("mem", 2)] + [("ml_n0", h) for h in range(4)]
       + [("fx_o", h) for h in range(8)] + [("ml_y", 2)] + [("ca_o", h) for h in range(4)]
       + [("moe", 2)],
    7: [("rows", 0), ("x", 3), ("mem", 3)] + [("ml_n1", h) for h in range(4)] + [("ml_y", 3)],
}


OUT_BANKS = (4, 5, 6, 4)


def turn(bank, user):
    return BANK_USERS[bank].index(user) + 1


def act_drains(i):
    return sum(SLOTS[n][0] not in ON_DVE for n in range(i + 1))


def dve_drains(i):
    return sum(SLOTS[n][0] in ON_DVE for n in range(i + 1))


def build(nc, x, mem, norm_mix, w_in, b_ml_gates, conv_ml, ml_head_norm, b_fx_gate, norm_mem,
          w_mem_kv, w_branch, w_out, norm_moe, w_router, b_router, w_exp_in, b_exp_in,
          w_exp_out, b_exp_out, norm_final, out):
    ctx = ExitStack()
    with ctx:
        def sb(name, shape, dt=F32):
            return ctx.enter_context(nc.sbuf_tensor(name, shape, dt))

        def sem(name):
            return ctx.enter_context(nc.semaphore(name))

        bank = [ctx.enter_context(nc.psum_tensor(f"bank{b}", [P, 512], F32)) for b in range(8)]

        xs = sb("xs", [P, TT, D])
        fxqT = sb("fxqT", [P, KT, S])
        yfxT = fxqT
        fxkT = sb("fxkT", [P, KT, S])
        fxv = sb("fxv", [P, TT, D])
        mems = fxv
        big_c = sb("big_c", [P, KT * (S + 3)])
        pre = big_c[:, :].rearrange("p (c s) -> p c s", c=KT)
        b1rows = big_c[:, 0:2 * FF]
        gfin = sb("gfin", [P, D])

        ident = sb("ident", [P, P])
        before = sb("before", [P, P])
        ones = sb("ones", [P, P])
        slots_f = sb("slots_f", [P, CAP * ROUNDS + CAP])
        eps = sb("eps", [P, 1])
        warm_dump = sb("warm_dump", [P, 4])
        rows = sb("rows", [64, P])
        cols = sb("cols", [P, 64])
        g_mix, g_mem, g_moe, g_head = (cols[:, 8 * i:8 * i + 8] for i in range(4))
        conv_c = cols[:, 32:64].rearrange("p (j c) -> p j c", j=4)
        wg = sb("wg", [P, KT, 16])
        gtok = sb("gtok", [P, TT, 16])
        bF = sb("bF", [12, 1])
        bI = sb("bI", [4, 1])
        wr = sb("wr", [P, KT, NE])
        br = sb("br", [P, NE])
        ss = sb("ss", [P, 2, 4])
        sq = sb("sq", [P, 2])
        std = sb("std", [P, 2, 4])
        rstd = sb("rstd", [P, 2, 4])
        cF = sb("cF", [12, S])
        mrun = sb("mrun", [4, S])
        acol = sb("acol", [P, TT, 4])
        floor = sb("floor", [P, TT, 4])
        p_a = sb("p_a", [P, 512])
        p_b = sb("p_b", [P, 512])
        p_t = sb("p_t", [P, 512])
        negmax = sb("negmax", [P, 2])
        esum = sb("esum", [P, 2])
        rsum = sb("rsum", [P, 2])
        den = sb("den", [P, TT, 4])
        rden = sb("rden", [P, TT, 4])
        fac = sb("fac", [P, TT, 4])
        msq = sb("msq", [P, TT, 4])

        tT = fxqT
        tn = fxv
        b2rows = fxkT[:, :, :].rearrange("p c s -> p (c s)")[0:NE, 0:D]
        square_dump = [fxkT[:, 4 * t:4 * t + 4, :].rearrange("p c s -> p (c s)") for t in range(TT)]
        moe_a = fxqT[:, :, :].rearrange("p c s -> p (c s)")
        moe_b = fxkT[:, :, :].rearrange("p c s -> p (c s)")
        got = moe_a[:, 0:512]
        gotT = moe_a[:, 512:1024].rearrange("p (q h c) -> p q h c", q=4, h=2)
        aT = moe_a[:, 1024:1536].rearrange("p (q h c) -> p q h c", q=4, h=2)
        selWT = moe_a[:, 1536:1792].rearrange("p (t n) -> p t n", t=TT)
        gate, lin, sig, act_out = (moe_b[:, 512 * n:512 * (n + 1)] for n in range(4))
        weighted = [moe_a[:, 0:D], moe_a[:, D:2 * D]]
        yS = p_a[:, :]
        pick_e = sb("pick_e", [P, CAP])
        sel = sb("sel", [P, TT, CAP])
        selW = sb("selW", [P, TT, 2, CAP])
        logits = sb("logits", [P, TT, NE])
        top = sb("top", [P, TT, 8])
        topi = sb("topi", [P, TT, 8], U32)
        topf = sb("topf", [P, TT, 8])
        topw = sb("topw", [P, TT, TOPK])
        hot = p_b[:, 0:256].rearrange("p (t j e) -> p t j e", t=TT, j=TOPK)
        mask = sb("mask", [P, TT, NE])
        comb = sb("comb", [P, TT, NE + 2])
        rank = sb("rank", [P, TT, NE + 2])
        combT = p_b[0:NE, 256:512]
        most = sb("most", [P, 1], I32)

        mixing = ExitStack()

        def part(name, shape, dt=F32):
            return mixing.enter_context(nc.sbuf_tensor(name, shape, dt))

        ring = [part(f"ring{b}", [P, KT, UW]) for b in range(RING)]
        big_b = part("big_b", [P, 2 * D])
        caqT = big_b[:, :].rearrange("p (c s) -> p c s", c=KT)
        fpre, fabs, fexp, fln, lf, grow, arow_, mrow_ = (big_b[0:12, S * n:S * (n + 1)] for n in range(8))
        ipre = grow[0:4, :]
        arow = arow_[0:4, :]
        mrow = mrow_[0:4, :]
        big_e = part("big_e", [P, TT * ML_H * (ML_DV + 1)])
        mval = big_e[:, :].rearrange("p (t h v) -> p t h v", t=TT, h=ML_H)
        vm = big_e[:, 0:2 * D].rearrange("p (t d) -> p t d", t=TT)
        pick = part("pick", [12, 12, P])
        fxmask = part("fxmask", [P, 384])
        big_a = part("big_a", [P, 2 * (D + 4)])
        xn = big_a[:, 0:2 * D].rearrange("p (t d) -> p t d", t=TT)
        num = big_a[:, :].rearrange("p (t h v) -> p t h v", t=TT, h=ML_H)
        gsig = big_a[:, 0:2 * D].rearrange("p (c s) -> p c s", c=KT)
        big_f = part("big_f", [P, 2 * D])
        sig_o = big_f[:, :].rearrange("p (t d) -> p t d", t=TT)
        ycaT = big_f[:, :].rearrange("p (c s) -> p c s", c=KT)
        o_hi, o_lo = (part(f"o_{n}", [P, KT, S], F32R) for n in ("hi", "lo"))
        h_hi, h_lo = (part(f"h_{n}", [P, KT, S], F32R) for n in ("hi", "lo"))
        merged = part("merged", [P, KT, S])
        qkT, kmT = merged, merged
        w_hi = [part(f"w_hi{n}", [P, KT, HW], F32R) for n in range(2)]
        w_lo = [part(f"w_lo{n}", [P, KT, HW], F32R) for n in range(2)]
        mixing.close()

        place = [sb(f"place{b}", [P, KT // 2, 2 * UW]) for b in range(2 * W1 + W2)]
        w1_buf = [place[0:W1], place[W1 + W2:2 * W1 + W2]]
        w2_buf = place[W1:W1 + W2]

        weights_in = [sem(f"weights_in{b}") for b in range(RING)]
        first_half_in = sem("first_half_in")
        weights_rounded, weights_split = sem("weights_rounded"), sem("weights_split")
        w1_in = [[sem(f"w1_in{p}{j}") for j in range(W1)] for p in range(2)]
        w1_used = [[sem(f"w1_used{p}{j}") for j in range(W1)] for p in range(2)]
        w2_in = [sem(f"w2_in{j}") for j in range(W2)]
        w2_used = [sem(f"w2_used{j}") for j in range(W2)]
        o_rounded, o_split = sem("o_rounded"), sem("o_split")
        turned_rounded = sem("turned_rounded")
        scaled_act = sem("scaled_act")
        x_in = [sem(f"x_in{t}") for t in range(TT)]
        mem_in, rows_in, gatew_in, gateb_in = (sem(n) for n in ("mem_in", "rows_in", "gatew_in", "gateb_in"))
        router_in, b1_in, b2_in, final_in, out_sent = (sem(n) for n in ("router_in", "b1_in", "b2_in", "final_in", "out_sent"))
        consts = sem("consts")
        pool_step = sem("pool_step")
        proj_done = sem("proj_done")
        act_drained, dve_drained = sem("act_drained"), sem("dve_drained")
        filled = {b: sem(f"bank{b}_filled") for b in range(4, 8)}
        drained = {b: sem(f"bank{b}_drained") for b in range(4, 8)}
        squares = sem("squares")
        std_ready = sem("std_ready")
        scaled = sem("scaled")
        ml_ready = sem("ml_ready")
        pre_zero = sem("pre_zero")
        conv_sum, conv_sig, qk_ready = sem("conv_sum"), sem("conv_sig"), sem("qk_ready")
        gate_lin, gate_log, gates_ready = sem("gate_lin"), sem("gate_log"), sem("gates_ready")
        act_step = sem("act_step")
        col_ready = sem("col_ready")
        ml_arg, ml_exp, ml_masked = sem("ml_arg"), sem("ml_exp"), sem("ml_masked")
        ml_num, ml_ms, ml_std, ml_y = sem("ml_num"), sem("ml_ms"), sem("ml_std"), sem("ml_y")
        max_ready, exp_ready, prob_ready, pt_ready, y_ready = (sem(n) for n in ("max_ready", "exp_ready", "prob_ready", "pt_ready", "y_ready"))
        dve_step = sem("dve_step")
        tT_ready, logits_done, topm_ready, topw_exp = (sem(n) for n in ("tT_ready", "logits_done", "topm_ready", "topw_exp"))
        mask_ready, rank_done, route_ready, comb_turned, combT_ready = (sem(n) for n in ("mask_ready", "rank_done", "route_ready", "comb_turned", "combT_ready"))
        bias_done = sem("bias_done")
        sel_ready, selW_ready, gather_done, got_ready = (sem(n) for n in ("sel_ready", "selW_ready", "gather_done", "got_ready"))
        got_turned, gotT_ready, pick_ready, act_turned, act_ready = (sem(n) for n in ("got_turned", "gotT_ready", "pick_ready", "act_turned", "act_ready"))
        sq_ready, rstd_ready = sem("sq_ready"), sem("rstd_ready")
        b1_zero, round_end = sem("b1_zero"), sem("round_end")
        selT_done, selWT_ready = sem("selT_done"), sem("selWT_ready")
        gate_ready, sig_ready, ffn_step, aT_ready = (sem(n) for n in ("gate_ready", "sig_ready", "ffn_step", "aT_ready"))
        yS_ready, put_done, put_added = (sem(n) for n in ("yS_ready", "put_done", "put_added"))
        moe_end, final_std, final_sq = (sem(n) for n in ("moe_end", "final_std", "final_sq"))
        final_scaled, final_rstd = sem("final_scaled"), sem("final_rstd")
        final_ready = [sem(f"final_ready{t}") for t in range(TT)]

        block = ctx.enter_context(nc.Block())

        def unit_source(name, j):
            base = {"mlqk": C_QK, "mlv": C_V, "mlo": C_O, "fxq": C_FQ, "fxk": C_FK, "fxv": C_FV,
                    "caq": C_CQ, "g0": C_G, "g1": C_G + D, "g2": C_G + 2 * D}
            if name in base:
                m, c = w_in[0], base[name]
            elif name in ("mk", "mv"):
                m, c = w_mem_kv[0], D * (name == "mv")
            elif name == "out":
                m, c = w_out[0], 0
            else:
                m, c = w_branch[0, int(name[1])], 0
            return m[:, c + UW * j:c + UW * (j + 1)].rearrange("(k p) n -> p k n", p=P)

        def for_rounds(eng, body):
            eng.wait_ge(route_ready, 1)
            busiest = eng.value_load(most[0:1, 0:1], min_val=0, max_val=S)
            body(0, first=True)
            with eng.If(busiest > CAP):
                with eng.Fori(1, ROUNDS) as r:
                    with eng.If(busiest > r * CAP):
                        body(r)

        @block.sync
        def _(sp):
            for t in range(TT):
                sp.dma_start(xs[:, t, :], x[0, P * t:P * (t + 1), :]).then_inc(x_in[t], 16)
            sp.dma_start(rows[16:24, :], norm_moe[0].rearrange("(r n) -> r n", n=P)).then_inc(rows_in, 16)
            sp.dma_start(rows[24:32, :], ml_head_norm[0].rearrange("(r n) -> r n", n=P)).then_inc(rows_in, 16)
            sp.dma_start(rows[32:64, :], conv_ml[0].rearrange("j (r n) -> (j r) n", n=P)).then_inc(rows_in, 16)
            for u, (name, kind, j) in enumerate(UNITS):
                b = u % RING
                if u >= RING:
                    sp.wait_ge(weights_split, 2 * (u - RING) + 2)
                if u == 0:
                    src = unit_source(name, j)
                    sp.dma_start(ring[b][:, :, 0:HW], src[:, :, 0:HW]).then_inc(first_half_in, 16)
                    sp.dma_start(ring[b][:, :, HW:UW], src[:, :, HW:UW]).then_inc(weights_in[b], 16)
                else:
                    sp.dma_start(ring[b][:, :, :], unit_source(name, j)).then_inc(weights_in[b], 16)
                if u == 0:
                    wv = w_in[0].rearrange("(k p) n -> p k n", p=P)
                    sp.dma_start(wg[:, :, 0:4], wv[:, :, C_F:C_F + 4]).then_inc(gatew_in, 16)
                    sp.dma_start(wg[:, :, 4:12], wv[:, :, C_FF:C_FF + 8]).then_inc(gatew_in, 16)
                    sp.dma_start(wg[:, :, 12:16], wv[:, :, C_I:C_I + 4]).then_inc(gatew_in, 16)
                    sp.dma_start(bI[:, :], b_ml_gates[0, 0:4].rearrange("(a n) -> a n", n=1)).then_inc(gateb_in, 16)
                    sp.dma_start(bF[0:4, :], b_ml_gates[0, 4:8].rearrange("(a n) -> a n", n=1)).then_inc(gateb_in, 16)
                    sp.dma_start(bF[4:12, :], b_fx_gate[0].rearrange("(a n) -> a n", n=1)).then_inc(gateb_in, 16)
                if u == 1:
                    sp.dma_start(mems[:, :, :], mem[0].rearrange("(t p) d -> p t d", p=P)).then_inc(mem_in, 16)

            def load_w1(e, p, j):
                w = w_exp_in[0, e:e + 1] if isinstance(e, int) else w_exp_in[0, bass.ds(e, 1)]
                part_, low = j // 2, D // 2 * (j % 2)
                src = w[:, low:low + D // 2, FF * part_:FF * (part_ + 1)].rearrange("e (k p) n -> p (e k) n", p=P)
                sp.dma_start(w1_buf[p][j][:, :, :], src).then_inc(w1_in[p][j], 16)

            def load_w2(e, j):
                w = w_exp_out[0, e:e + 1] if isinstance(e, int) else w_exp_out[0, bass.ds(e, 1)]
                src = w[:, FF // 2 * j:FF // 2 * (j + 1), :].rearrange("e (k p) n -> p (e k) n", p=P)
                sp.dma_start(w2_buf[j][:, :, :], src).then_inc(w2_in[j], 16)

            def load_w1_after(pair, e, p):
                for j in range(W1):
                    sp.wait_ge(w1_used[p][j], pair)
                    load_w1(e, p, j)

            def load_w2_after(n, e):
                for j in range(W2):
                    sp.wait_ge(w2_used[j], n)
                    load_w2(e, j)

            def load_pair(pair, e):
                for p in range(2):
                    load_w1_after(pair, e + p, p)
                    load_w2_after(pair * 2 + p, e + p)

            sp.wait_ge(proj_done, FIRST["caq"] + 11)
            for j in range(RING, W1):
                load_w1(0, 0, j)
            sp.wait_ge(dve_drained, dve_drains(FIRST["b2"] + 3))
            sp.wait_ge(proj_done, FIRST["b2"] + 4)
            for j in range(W2):
                load_w2(0, j)
            for u in range(len(UNITS) - RING, len(UNITS)):
                sp.wait_ge(weights_split, 2 * u + 2)
                load_w1(0, 0, u % RING)
            sp.wait_ge(proj_done, len(SLOTS))
            for j in range(W1):
                load_w1(1, 1, j)
            with sp.Fori(0, AHEAD) as m:
                for p in range(2):
                    load_w1_after(m + 1, m * 2 + 2 + p, p)
                    load_w2_after(m * 2 + 1 + p, m * 2 + 1 + p)
            load_w2_after(2 * AHEAD + 1, 2 * AHEAD + 1)
            with sp.Fori(AHEAD + 1, NE // 2) as m:
                load_pair(m, m * 2)
            sp.wait_ge(route_ready, 1)
            busiest = sp.value_load(most[0:1, 0:1], min_val=0, max_val=S)
            with sp.If(busiest > CAP):
                with sp.Fori(1, ROUNDS) as r:
                    with sp.If(busiest > r * CAP):
                        with sp.Fori(0, NE // 2) as m:
                            load_pair(r * (NE // 2) + m, m * 2)
            for t in range(TT):
                sp.wait_ge(final_ready[t], 1)
                sp.dma_start(out[0].rearrange("(t p) d -> p t d", p=P)[:, t, :], tn[:, t, :]).then_inc(out_sent, 16)
            sp.wait_ge(out_sent, 16 * TT)

        @block.gpsimd
        def _(pool):
            pool.memset(eps[:, :], EPS).then_inc(consts, 1)
            pool.memset(ident[:, :], 0.0).then_inc(pool_step, 1)
            pool.memset(before[:, :], 1.0).then_inc(pool_step, 1)
            pool.memset(fxmask[:, :], 0.0).then_inc(pool_step, 1)
            pool.memset(pick[:, :, :], 0.0).then_inc(pool_step, 1)
            pool.memset(ones[:, :], 1.0).then_inc(consts, 1)
            pool.memset(mval[:, :, :, ML_DV:ML_DV + 1], 1.0).then_inc(consts, 1)
            pool.wait_ge(pool_step, 4)
            pool.affine_select(out=ident[:, :], in_=ident[:, :], compare_op=ALU.not_equal, fill=1.0,
                               base=0, pattern=[[-1, P]], channel_multiplier=1).then_inc(consts, 1)
            pool.affine_select(out=before[:, :], in_=before[:, :], compare_op=ALU.is_gt, fill=0.0,
                               base=0, pattern=[[1, P]], channel_multiplier=-1).then_inc(consts, 1)
            pool.affine_select(out=pick[:, :, :], in_=pick[:, :, :], compare_op=ALU.not_equal, fill=-1.0,
                               base=0, pattern=[[-1, 12], [0, P]], channel_multiplier=1).then_inc(consts, 1)
            for c in (0, 256):
                pool.affine_select(out=fxmask[:, c:c + P], in_=fxmask[:, c:c + P], compare_op=ALU.is_ge,
                                   fill=-1e30, base=0, pattern=[[-1, P]], channel_multiplier=1).then_inc(consts, 1)
            pool.iota(slots_f[:, :], [[1, CAP * (ROUNDS + 1)]], base=0, channel_multiplier=0,
                      allow_small_or_imprecise_dtypes=True).then_inc(consts, 1)
            for h in range(ML_H):
                pool.wait_ge(ml_exp, h + 1)
                for n, c in enumerate((0, 256)):
                    pool.affine_select(out=p_b[:, c:c + P], in_=p_b[:, c:c + P], compare_op=ALU.is_ge,
                                       fill=0.0, base=0, pattern=[[1, P]],
                                       channel_multiplier=-1).then_inc(ml_masked, 1)
            pool.wait_ge(qk_ready, 4)
            pool.memset(b1rows, 0.0).then_inc(b1_zero, 1)

        ALL_CONSTS = 9

        @block.scalar
        def _(act):
            act.dma_start(rows[0:8, :], norm_mix[0].rearrange("(r n) -> r n", n=P)).then_inc(rows_in, 16)
            act.dma_start(rows[8:16, :], norm_mem[0].rearrange("(r n) -> r n", n=P)).then_inc(rows_in, 16)
            warmed = [0]

            def warm(fun):
                act.activation(warm_dump[:, warmed[0]:warmed[0] + 1], eps[:, :], fun)
                warmed[0] += 1

            def square_sums(src, n, loaded):
                for t in range(TT):
                    act.wait_ge(loaded[t], 16)
                    act.activation(square_dump[t], src[:, t, :], ACT.Square, accum_out=ss[:, t, 0:1]).then_inc(squares, 1)
                act.wait_ge(squares, 2 * n + 2)
                act.activation(std[:, :, 0:1], ss[:, :, 0:1], ACT.Sqrt, bias=eps[:, 0:1],
                               scale=1.0 / D).then_inc(std_ready, 1)

            def round_turned(hi, user, g):
                for q in range(4):
                    act.wait_ge(filled[4 + q], turn(4 + q, (user, q)))
                    for c in range(2):
                        ins = act.activation(hi[:, 2 * q + c, :], bank[4 + q][:, S * c:S * (c + 1)], ACT.Copy,
                                             scale=g[:, 2 * q + c:2 * q + c + 1])
                    ins.then_inc(turned_rounded, 1)

            def round_weights(i):
                if i >= len(SLOTS):
                    return
                u = i // 2
                if i == 0:
                    act.wait_ge(first_half_in, 16)
                else:
                    act.wait_ge(weights_in[u % RING], 16 * (u // RING + 1))
                if i >= 2:
                    act.wait_ge(proj_done, i - 1)
                act.activation(w_hi[i % 2][:, :, :], ring[u % RING][:, :, HW * (i % 2):HW * (i % 2 + 1)],
                               ACT.Copy).then_inc(weights_rounded, 1)

            act.wait_ge(consts, 1)
            warm(ACT.Sqrt)
            square_sums(xs, 0, x_in)
            round_weights(0)
            act.wait_ge(drained[7], 1)
            round_turned(h_hi, "x", g_mix)
            round_weights(1)
            act.wait_ge(scaled, 2)
            square_sums(mems, 1, [mem_in, mem_in])

            def drain(i):
                name, kind, j, half = SLOTS[i]
                if name in ON_DVE:
                    return
                act.wait_ge(proj_done, i + 1)
                src = pair = bank[i % 4][:, :].rearrange("p (c s) -> p c s", c=2)
                c0, col = 4 * j + 2 * half, UW * j + HW * half
                fun, scale = ACT.Copy, 1.0
                if name == "mlqk":
                    dst, src = pre[:, c0:c0 + 2, 3:S + 3], pair
                elif name == "mlv":
                    dst = mval[:, :, 2 * j + half, 0:ML_DV]
                elif name == "mlo":
                    dst, fun = sig_o[:, :, col:col + HW], ACT.Sigmoid
                elif name == "fxq":
                    dst, src, scale = fxqT[:, c0:c0 + 2, :], pair, FX_SCALE
                elif name == "fxk":
                    dst, src = fxkT[:, c0:c0 + 2, :], pair
                elif name == "fxv":
                    dst = fxv[:, :, col:col + HW]
                elif name == "mk":
                    dst, src = kmT[:, c0:c0 + 2, :], pair
                elif name == "mv":
                    dst = vm[:, :, col:col + HW]
                elif name == "caq":
                    dst, src = caqT[:, c0:c0 + 2, :], pair
                else:
                    if name in ("g1", "g2"):
                        act.wait_ge(dve_drained, 4 * int(name[1]))
                    dst, src, fun = gsig[:, c0:c0 + 2, :], pair, ACT.Sigmoid
                act.activation(dst, src, fun, scale=scale).then_inc(act_drained, 1)

            def conv_silu(i):
                act.wait_ge(conv_sum, 8 * (i + 1))
                act.activation(p_b[:, :], p_a[:, :], ACT.Sigmoid).then_inc(conv_sig, 1)

            def gate_logs():
                act.wait_ge(gate_lin, 1)
                act.activation(fabs, fpre, ACT.Abs).then_inc(act_step, 1)
                act.wait_ge(act_step, 1)
                act.activation(fexp, fabs, ACT.Exp, scale=-1.0).then_inc(act_step, 1)
                act.wait_ge(act_step, 2)
                act.activation(fln, fexp, ACT.Ln, bias=1.0).then_inc(gate_log, 1)

            def gate_columns():
                act.wait_ge(filled[5], turn(5, ("gcol", 0)))
                col = bank[5][:, 0:16].rearrange("p (w t h) -> p w t h", w=2, t=TT)
                act.activation(acol[:, :, :], col[:, 0], ACT.Copy)
                act.activation(floor[:, :, :], col[:, 1], ACT.Exp, scale=-1.0).then_inc(drained[5], 1)

            def ml_scores(h):
                act.wait_ge(ml_arg, h + 1)
                act.wait_ge(drained[5], turn(5, ("ml_m", h)))
                if h:
                    act.wait_ge(drained[4], turn(4, ("ml_s", h - 1)))
                act.activation(p_b[:, 0:384], p_a[:, 0:384], ACT.Exp).then_inc(ml_exp, 1)

            def ml_values(h):
                for t in range(TT):
                    act.wait_ge(filled[6 + t], turn(6 + t, (f"ml_n{t}", h)))
                    act.activation(p_scr[ML_H * t + h], bank[6 + t][:, 0:ML_DV], ACT.Square,
                                   accum_out=ss[:, t, h:h + 1]).then_inc(ml_num, 1)
                    act.activation(num[:, t, h, :], bank[6 + t][:, 0:ML_DV + 1],
                                   ACT.Copy).then_inc(drained[6 + t], 1)

            p_scr = [fxv[:, t, ML_DV * h:ML_DV * (h + 1)] for t in range(TT) for h in range(ML_H)]

            def ml_norm():
                act.wait_ge(ml_ms, 1)
                act.activation(std[:, :, :], msq[:, :, :], ACT.Sqrt, bias=eps[:, 0:1],
                               scale=1.0 / ML_DV).then_inc(ml_std, 1)

            def fx_scores(h):
                act.wait_ge(max_ready, h + 1)
                if h:
                    act.wait_ge(filled[5], turn(5, ("fx_p", h - 1)))
                act.activation(p_b[:, 0:128], p_a[:, 0:128], ACT.Exp, bias=negmax[:, 0:1],
                               accum_out=esum[:, 0:1]).then_inc(exp_ready, 1)
                act.activation(p_b[:, 128:384], p_a[:, 128:384], ACT.Exp, bias=negmax[:, 1:2],
                               accum_out=esum[:, 1:2]).then_inc(exp_ready, 1)

            def fx_turn(h):
                act.wait_ge(filled[5], turn(5, ("fx_p", h)))
                if h:
                    act.wait_ge(filled[6], turn(6, ("fx_o", h - 1)))
                act.activation(p_t[:, 0:384], bank[5][:, 0:384], ACT.Copy).then_inc(drained[5], 1)

            def fx_values(h):
                act.wait_ge(filled[6], turn(6, ("fx_o", h)))
                act.activation(yfxT[:, h, :], bank[6][:, 0:S], ACT.Copy).then_inc(drained[6], 1)

            def ca_scores(h):
                act.wait_ge(max_ready, FX_H + h + 1)
                if h:
                    act.wait_ge(filled[5], turn(5, ("ca_p", h - 1)))
                for t in range(TT):
                    ins = act.activation(p_b[:, S * t:S * (t + 1)], bank[4][:, S * t:S * (t + 1)], ACT.Exp,
                                         bias=negmax[:, t:t + 1], scale=CA_SCALE, accum_out=esum[:, t:t + 1])
                    ins.then_inc(drained[4] if t else exp_ready, 1)

            def ca_turn(h):
                act.wait_ge(filled[5], turn(5, ("ca_p", h)))
                if h:
                    act.wait_ge(filled[6], turn(6, ("ca_o", h - 1)))
                act.activation(p_t[:, :], bank[5][:, :], ACT.Copy).then_inc(drained[5], 1)

            def ca_values(h):
                act.wait_ge(filled[6], turn(6, ("ca_o", h)))
                act.activation(ycaT[:, 2 * h:2 * h + 2, :], bank[6][:, :].rearrange("p (c s) -> p c s", c=2),
                               ACT.Copy).then_inc(drained[6], 1)

            def mem_turn():
                round_turned(o_hi, "mem", g_mem)

            def ml_turn():
                act.wait_ge(proj_done, FIRST["mv"] + 4)
                round_turned(o_hi, "ml_y", g_head)

            def split_fx():
                act.wait_ge(proj_done, FIRST["b0"] + 4)
                act.activation(o_hi[:, :, :], yfxT[:, :, :], ACT.Copy).then_inc(o_rounded, 1)

            def split_ca():
                act.wait_ge(proj_done, FIRST["b1"] + 4)
                act.activation(o_hi[:, :, :], ycaT[:, :, :], ACT.Copy).then_inc(o_rounded, 1)

            def square_out(q):
                act.wait_ge(dve_drained, dve_drains(FIRST["out"] + q))
                for t in range(TT):
                    act.activation(sq_dump[:, t, q, :], xs[:, t, HW * q:HW * (q + 1)], ACT.Square,
                                   accum_out=ss[:, t, q:q + 1]).then_inc(squares, 1)

            sq_dump = fxv[:, :, :].rearrange("p t (q c) -> p t q c", q=4)

            work = dict(conv_silu=conv_silu, gate_logs=gate_logs, gate_columns=gate_columns, mem_turn=mem_turn, ml_turn=ml_turn,
                        split_fx=split_fx, split_ca=split_ca, ml_scores=ml_scores,
                        ml_values=ml_values, ml_norm=ml_norm, fx_scores=fx_scores, fx_turn=fx_turn,
                        fx_values=fx_values, ca_scores=ca_scores, ca_turn=ca_turn,
                        ca_values=ca_values)
            for i in range(len(SLOTS)):
                if i != LAST_B2:
                    round_weights(i + 2)
                drain(i)
                if SLOTS[i][0] == "b2":
                    act.wait_ge(dve_drained, dve_drains(i))
                    c0 = 2 * (i - FIRST["b2"])
                    act.activation(h_hi[:, c0:c0 + 2, :], merged[:, c0:c0 + 2, :], ACT.Copy).then_inc(o_rounded, 1)
                if i == LAST_B2:
                    round_weights(i + 2)
                    warm(ACT.Sqrt)
                for name, *arg in STAGES.get(i, []):
                    if name in work:
                        work[name](*arg)
                if i > FIRST["out"]:
                    square_out(i - FIRST["out"] - 1)
                if i == 0:
                    act.dma_start(wr[:, :, :], w_router[0].rearrange("(k p) e -> p k e", p=P)).then_inc(router_in, 16)
                    act.dma_start(br[:, :], b_router[0].partition_broadcast(P)).then_inc(router_in, 16)
                if i == 44:
                    act.wait_ge(proj_done, 45)
                    act.dma_start(gfin[:, :], norm_final.partition_broadcast(P)).then_inc(final_in, 16)
                    act.dma_start(b2rows, b_exp_out[0]).then_inc(b2_in, 16)
                    act.wait_ge(b1_zero, 1)
                    act.dma_start(b1rows[0:NE, :], b_exp_in[0]).then_inc(b1_in, 16)

            square_out(3)
            act.wait_ge(sq_ready, 1)
            act.activation(std[:, :, 0:1].rearrange("p t o -> p (t o)"), sq[:, :], ACT.Sqrt, bias=eps[:, 0:1],
                           scale=1.0 / D).then_inc(std_ready, 1)
            warm(ACT.Exp)
            act.wait_ge(topm_ready, 1)
            for t in range(TT):
                act.activation(topw[:, t, :], top[:, t, 0:TOPK], ACT.Exp, bias=negmax[:, t:t + 1],
                               accum_out=esum[:, t:t + 1]).then_inc(topw_exp, 1)
            act.activation(tn[:, 1, :], xs[:, 1, :], ACT.Copy, scale=rstd[:, 1, 0:1]).then_inc(scaled_act, 1)

            def keep_gathered(k):
                act.wait_ge(gather_done, k)
                act.activation(got, bank[2][:, :], ACT.Copy).then_inc(got_ready, 1)

            def expert(r, n):
                act.wait_ge(gate_ready, n + 1)
                act.activation(sig, gate, ACT.Sigmoid, scale=ALPHA).then_inc(sig_ready, 1)
                keep_gathered(n + r + 2)
                act.wait_ge(selT_done, n + 1)
                act.activation(selWT, bank[6][:, 0:S].rearrange("p (t n) -> p t n", t=TT),
                               ACT.Copy).then_inc(selWT_ready, 1)
                act.wait_ge(act_turned, n + 1)
                act.activation(aT, bank[4][:, :].rearrange("p (q h c) -> p q h c", q=4, h=2),
                               ACT.Copy).then_inc(aT_ready, 1)
                act.wait_ge(w2_used[1], n + 1)
                act.activation(yS, bank[5][:, :], ACT.Copy).then_inc(yS_ready, 1)

            def experts(r, first=False):
                keep_gathered(r * (NE + 1) + 1)
                if first:
                    act.wait_ge(comb_turned, 1)
                    act.activation(combT, bank[7][0:NE, 0:S], ACT.Copy).then_inc(combT_ready, 1)
                with act.Fori(0, NE // 2) as m:
                    for p in range(2):
                        expert(r, r * NE + m * 2 + p)
                act.wait_ge(got_ready, (r + 1) * (NE + 1))
                act.sem_inc(round_end, 1)

            for_rounds(act, experts)
            warm(ACT.Sqrt)
            act.wait_ge(moe_end, 1)
            for t in range(TT):
                act.activation(b1rows[:, D * t:D * (t + 1)], xs[:, t, :], ACT.Square, accum_out=ss[:, t, 0:1]).then_inc(final_sq, 1)
            act.wait_ge(final_sq, 2)
            act.activation(std[:, :, 0:1], ss[:, :, 0:1], ACT.Sqrt, bias=eps[:, 0:1], scale=1.0 / D).then_inc(final_std, 1)
            act.wait_ge(final_scaled, 2)
            act.wait_ge(final_rstd, 1)
            act.activation(tn[:, 1, :], weighted[1], ACT.Copy, scale=rstd[:, 1, 0:1]).then_inc(final_ready[1], 1)

        @block.vector
        def _(dve):
            steps = [0]

            def step(ins):
                steps[0] += 1
                ins.then_inc(dve_step, 1)
                dve.wait_ge(dve_step, steps[0])

            def scale_rows(src, dst, n):
                dve.wait_ge(std_ready, n + 1)
                step(dve.reciprocal(rstd[:, :, 0:1], std[:, :, 0:1]))
                for t in range(TT):
                    dve.tensor_scalar(dst[:, t, :], src[:, t, :], rstd[:, t, 0:1], None, ALU.mult).then_inc(scaled, 1)

            def split_turned(hi, lo, user, g, done):
                for q in range(4):
                    dve.wait_ge(turned_rounded, 4 * done + q + 1)
                    for c in range(2):
                        ins = dve.scalar_tensor_tensor(
                            out=lo[:, 2 * q + c, :], in0=bank[4 + q][:, S * c:S * (c + 1)],
                            scalar=g[:, 2 * q + c:2 * q + c + 1], in1=hi[:, 2 * q + c, :].bitcast(F32),
                            op0=ALU.mult, op1=ALU.subtract)
                    ins.then_inc(drained[4 + q], 1)

            def split_weights(i):
                if i >= len(SLOTS):
                    return
                dve.wait_ge(weights_rounded, i + 1)
                dve.tensor_tensor(w_lo[i % 2][:, :, :], ring[i // 2 % RING][:, :, HW * (i % 2):HW * (i % 2 + 1)],
                                  w_hi[i % 2][:, :, :].bitcast(F32), ALU.subtract).then_inc(weights_split, 1)

            dve.memset(pre[:, :, 0:3], 0.0).then_inc(pre_zero, 1)
            scale_rows(xs, xn, 0)
            dve.wait_ge(filled[7], turn(7, ("rows", 0)))
            dve.tensor_copy(cols[:, :], bank[7][:, 0:64]).then_inc(drained[7], 1)
            dve.wait_ge(drained[7], 1)
            split_weights(0)
            split_turned(h_hi, h_lo, "x", g_mix, 0)
            split_weights(1)

            def drain(i):
                name, kind, j, half = SLOTS[i]
                if name not in ON_DVE:
                    return
                dve.wait_ge(proj_done, i + 1)
                if name == "out":
                    cut = xs[:, :, UW * j + HW * half:UW * j + HW * (half + 1)]
                    dve.tensor_tensor(cut, bank[i % 4][:, :].rearrange("p (t c) -> p t c", t=TT), cut,
                                      ALU.add).then_inc(dve_drained, 1)
                    return
                c0 = 4 * j + 2 * half
                pair = bank[i % 4][:, :].rearrange("p (c s) -> p c s", c=2)
                if c0 == 0:
                    dve.wait_ge(act_drained, act_drains(i))
                if name == "b0":
                    dve.tensor_tensor(merged[:, c0:c0 + 2, :], pair, gsig[:, c0:c0 + 2, :], ALU.mult).then_inc(dve_drained, 1)
                    return
                step(dve.tensor_tensor(gsig[:, c0:c0 + 2, :], pair, gsig[:, c0:c0 + 2, :], ALU.mult))
                dve.tensor_tensor(merged[:, c0:c0 + 2, :], merged[:, c0:c0 + 2, :], gsig[:, c0:c0 + 2, :],
                                  ALU.add).then_inc(dve_drained, 1)

            def conv(i):
                dve.wait_ge(act_drained, i + 1)
                if i == 0:
                    dve.wait_ge(pre_zero, 1)
                else:
                    dve.wait_ge(qk_ready, i)
                for tap in range(4):
                    for c in range(2):
                        a = p_a[:, S * c:S * (c + 1)]
                        src = pre[:, 2 * i + c, tap:tap + S]
                        w = conv_c[:, tap, 2 * i + c:2 * i + c + 1]
                        if tap == 0:
                            ins = dve.tensor_scalar(a, src, w, None, ALU.mult)
                        else:
                            ins = dve.scalar_tensor_tensor(out=a, in0=src, scalar=w, in1=a, op0=ALU.mult, op1=ALU.add)
                        ins.then_inc(conv_sum, 1)
                    dve.wait_ge(conv_sum, 8 * i + 2 * tap + 2)

            def conv_silu(i):
                dve.wait_ge(conv_sig, i + 1)
                dve.tensor_tensor(qkT[:, 2 * i:2 * i + 2, :], p_a[:, :].rearrange("p (c s) -> p c s", c=2),
                                  p_b[:, :].rearrange("p (c s) -> p c s", c=2), ALU.mult).then_inc(qk_ready, 1)

            def gate_tokens():
                dve.wait_ge(filled[4], turn(4, ("gtok", 0)))
                dve.tensor_copy(gtok[:, :, :], bank[4][:, 0:16 * TT].rearrange("p (t g) -> p t g", t=TT)).then_inc(drained[4], 1)

            def gates():
                dve.wait_ge(gateb_in, 48)
                dve.wait_ge(filled[4], turn(4, ("gates", 0)))
                step(dve.tensor_scalar(ipre, bank[4][0:4, S:2 * S], bI[:, 0:1], None, ALU.add))
                dve.tensor_scalar(fpre, bank[4][0:12, 0:S], bF[:, 0:1], None, ALU.add).then_inc(gate_lin, 1)

            def gate_sums():
                dve.wait_ge(gate_lin, 1)
                dve.wait_ge(gate_log, 1)
                step(dve.scalar_tensor_tensor(out=lf, in0=fpre, scalar=0.0, in1=fln,
                                              op0=ALU.min, op1=ALU.subtract))
                dve.wait_ge(consts, ALL_CONSTS)
                step(dve.memset(fabs, 1.0))
                step(dve.tensor_tensor_scan(cF[:, :], fabs, lf, 0.0, ALU.mult, ALU.add))
                step(dve.tensor_tensor(arow[:, :], ipre, cF[0:4, :], ALU.subtract))
                step(dve.tensor_tensor_scan(mrun[:, :], arow[:, :], arow[:, :], 0.0, ALU.max, ALU.max))
                dve.tensor_tensor(mrow[:, :], mrun[:, :], cF[0:4, :], ALU.add).then_inc(drained[4], 1)

            def mem_turn():
                split_turned(o_hi, o_lo, "mem", g_mem, 1)

            def ml_scores(h):
                dve.wait_ge(filled[5], turn(5, ("ml_m", h)))
                if h == 0:
                    dve.wait_ge(drained[5], turn(5, ("gcol", 0)))
                dve.tensor_scalar(p_a[:, 0:256], bank[5][:, 0:256], acol[:, 0, h:h + 1], 0.0,
                                  ALU.add, ALU.min).then_inc(ml_arg, 1)
                dve.tensor_scalar(p_a[:, 256:384], bank[5][:, 256:384], acol[:, 1, h:h + 1], 0.0,
                                  ALU.add, ALU.min).then_inc(drained[5], 1)
                dve.wait_ge(ml_masked, 2 * h + 2)
                dve.wait_ge(filled[4], turn(4, ("ml_s", h)))
                if h:
                    dve.wait_ge(filled[7], turn(7, ("ml_n1", h - 1)))
                dve.scalar_tensor_tensor(out=p_t[:, 0:384], in0=bank[4][:, 0:384], scalar=ML_SCALE,
                                         in1=p_b[:, 0:384], op0=ALU.mult, op1=ALU.mult).then_inc(drained[4], 1)

            def ml_norm():
                dve.wait_ge(drained[6], turn(6, ("ml_n0", 3)))
                dve.wait_ge(drained[7], turn(7, ("ml_n1", 3)))
                dve.wait_ge(ml_num, 8)
                step(dve.tensor_scalar(den[:, :, :], num[:, :, :, ML_DV:ML_DV + 1].rearrange("p t h o -> p t (h o)"),
                                       -1.0, None, ALU.mult))
                step(dve.tensor_tensor(den[:, :, :], num[:, :, :, ML_DV:ML_DV + 1].rearrange("p t h o -> p t (h o)"),
                                       den[:, :, :], ALU.max))
                step(dve.tensor_tensor(den[:, :, :], den[:, :, :], floor[:, :, :], ALU.max))
                step(dve.reciprocal(rden[:, :, :], den[:, :, :]))
                step(dve.tensor_tensor(msq[:, :, :], ss[:, :, :], rden[:, :, :], ALU.mult))
                dve.tensor_tensor(msq[:, :, :], msq[:, :, :], rden[:, :, :], ALU.mult).then_inc(ml_ms, 1)
                dve.wait_ge(ml_std, 1)
                step(dve.reciprocal(fac[:, :, :], std[:, :, :]))
                step(dve.tensor_tensor(fac[:, :, :], fac[:, :, :], rden[:, :, :], ALU.mult))
                dve.wait_ge(act_drained, act_drains(FIRST["mlo"] + 3))
                for t in range(TT):
                    for h in range(ML_H):
                        v = num[:, t, h, 0:ML_DV]
                        dve.scalar_tensor_tensor(out=v, in0=v, scalar=fac[:, t, h:h + 1],
                                                 in1=sig_o[:, t, ML_DV * h:ML_DV * (h + 1)],
                                                 op0=ALU.mult, op1=ALU.mult).then_inc(ml_y, 1)

            def ml_turn():
                split_turned(o_hi, o_lo, "ml_y", g_head, 2)

            def split_fx():
                dve.wait_ge(o_rounded, 1)
                dve.tensor_tensor(o_lo[:, :, :], yfxT[:, :, :], o_hi[:, :, :].bitcast(F32), ALU.subtract).then_inc(o_split, 1)

            def split_ca():
                dve.wait_ge(o_rounded, 2)
                dve.tensor_tensor(o_lo[:, :, :], ycaT[:, :, :], o_hi[:, :, :].bitcast(F32), ALU.subtract).then_inc(o_split, 1)

            def turn_out(q):
                b = OUT_BANKS[q]
                dve.wait_ge(filled[b], turn(b, ("moe", q)))
                for c in range(2):
                    ins = dve.tensor_scalar(tT[:, 2 * q + c, :], bank[b][:, S * c:S * (c + 1)],
                                            g_moe[:, 2 * q + c:2 * q + c + 1], None, ALU.mult)
                ins.then_inc(drained[b], 1)

            def normalise(cuts):
                step(dve.reciprocal(rsum[:, :], esum[:, :]))
                for t, (a, b) in enumerate(cuts):
                    dve.tensor_scalar(p_b[:, a:b], p_b[:, a:b], rsum[:, t:t + 1], None, ALU.mult).then_inc(prob_ready, 1)

            def fx_scores(h):
                dve.wait_ge(filled[4], turn(4, ("fx_s", h)))
                dve.tensor_tensor(p_a[:, 0:384], bank[4][:, 0:384], fxmask[:, :], ALU.add).then_inc(drained[4], 1)
                dve.wait_ge(drained[4], turn(4, ("fx_s", h)))
                step(dve.tensor_reduce(negmax[:, 0:1], p_a[:, 0:128], AX.X, ALU.max, negate=True))
                dve.tensor_reduce(negmax[:, 1:2], p_a[:, 128:384], AX.X, ALU.max, negate=True).then_inc(max_ready, 1)
                dve.wait_ge(exp_ready, 2 * h + 2)
                normalise(((0, 128), (128, 384)))

            def ca_scores(h):
                dve.wait_ge(filled[4], turn(4, ("ca_s", h)))
                step(dve.tensor_reduce(negmax[:, :], bank[4][:, :].rearrange("p (t m) -> p t m", t=TT), AX.X, ALU.max))
                dve.tensor_scalar(negmax[:, :], negmax[:, :], -CA_SCALE, None, ALU.mult).then_inc(max_ready, 1)
                dve.wait_ge(exp_ready, 2 * FX_H + h + 1)
                dve.wait_ge(drained[4], turn(4, ("ca_s", h)))
                normalise(((0, 256), (256, 512)))

            work = dict(conv=conv, conv_silu=conv_silu, gate_tokens=gate_tokens, gates=gates, gate_sums=gate_sums, mem_turn=mem_turn,
                        ml_scores=ml_scores, ml_norm=ml_norm,
                        ml_turn=ml_turn, fx_scores=fx_scores, ca_scores=ca_scores, split_fx=split_fx,
                        split_ca=split_ca, turn_out=turn_out)
            for i in range(len(SLOTS)):
                if SLOTS[i][0] in ON_DVE:
                    drain(i)
                if i != LAST_B2:
                    split_weights(i + 2)
                if SLOTS[i][0] == "b2":
                    c0 = 2 * (i - FIRST["b2"])
                    dve.wait_ge(o_rounded, 3 + i - FIRST["b2"])
                    dve.tensor_tensor(h_lo[:, c0:c0 + 2, :], merged[:, c0:c0 + 2, :],
                                      h_hi[:, c0:c0 + 2, :].bitcast(F32), ALU.subtract).then_inc(o_split, 1)
                if i == LAST_B2:
                    split_weights(i + 2)
                for name, *arg in STAGES.get(i, []):
                    if name in work:
                        work[name](*arg)
                if i == 1:
                    scale_rows(mems, xn, 1)

            turn_out(3)
            dve.wait_ge(squares, 2 * 2 + 2 * 4)
            dve.tensor_reduce(sq[:, :], ss[:, :, :], AX.X, ALU.add).then_inc(sq_ready, 1)
            dve.wait_ge(std_ready, 3)
            dve.reciprocal(rstd[:, :, 0:1], std[:, :, 0:1]).then_inc(rstd_ready, 1)
            dve.wait_ge(rstd_ready, 1)
            dve.wait_ge(router_in, 32)
            for t in range(TT):
                dve.wait_ge(logits_done, t + 1)
                step(dve.scalar_tensor_tensor(out=logits[:, t, :], in0=bank[t][:, 0:NE], scalar=rstd[:, t, 0:1],
                                              in1=br[:, :], op0=ALU.mult, op1=ALU.add))
                step(dve.max(top[:, t, :], logits[:, t, :]))
                step(dve.max_index(topi[:, t, :], top[:, t, :], logits[:, t, :]))
            step(dve.tensor_copy(topf[:, :, :], topi[:, :, :]))
            dve.tensor_scalar(negmax[:, :], top[:, :, 0:1].rearrange("p t o -> p (t o)"), -1.0, None,
                              ALU.mult).then_inc(topm_ready, 1)
            step(dve.tensor_tensor(hot[:, 0], slots_f[:, 0:NE].unsqueeze(1).to_broadcast([P, TOPK, NE]),
                                   topf[:, 0, 0:TOPK].unsqueeze(2).to_broadcast([P, TOPK, NE]), ALU.is_equal))
            step(dve.tensor_tensor(hot[:, 1], slots_f[:, 0:NE].unsqueeze(1).to_broadcast([P, TOPK, NE]),
                                   topf[:, 1, 0:TOPK].unsqueeze(2).to_broadcast([P, TOPK, NE]), ALU.is_equal))
            dve.tensor_reduce(mask[:, :, :], hot[:, :, :, :].rearrange("p t j e -> p t e j"), AX.X,
                              ALU.add).then_inc(mask_ready, 1)
            dve.tensor_scalar(tn[:, 0, :], xs[:, 0, :], rstd[:, 0, 0:1], None, ALU.mult).then_inc(scaled, 1)
            dve.memset(comb[:, :, NE:NE + 2], 0.0)
            step(dve.memset(rank[:, :, NE:NE + 2], -1.0))
            dve.wait_ge(topw_exp, 2)
            step(dve.reciprocal(rsum[:, :], esum[:, :]))
            dve.wait_ge(mask_ready, 1)
            for t in range(TT):
                step(dve.tensor_scalar(topw[:, t, :], topw[:, t, :], rsum[:, t:t + 1], None, ALU.mult))
                step(dve.tensor_tensor(hot[:, t], hot[:, t], topw[:, t, :].unsqueeze(2).to_broadcast([P, TOPK, NE]),
                                       ALU.mult))
            step(dve.tensor_reduce(comb[:, :, 0:NE], hot[:, :, :, :].rearrange("p t j e -> p t e j"), AX.X, ALU.add))
            dve.wait_ge(rank_done, 1)
            counts = bank[3][:, 128:192].rearrange("p (t e) -> p t e", t=TT)
            step(dve.scalar_tensor_tensor(out=rank[:, :, 0:NE], in0=counts, scalar=1.0, in1=mask[:, :, :],
                                          op0=ALU.add, op1=ALU.mult))
            step(dve.tensor_scalar(rank[:, :, 0:NE], rank[:, :, 0:NE], 1.0, None, ALU.subtract))
            dve.tensor_reduce(most[:, :], bank[3][:, 192:224], AX.X, ALU.max).then_inc(route_ready, 1)

            def add_biases():
                for q in range(4):
                    t, c = q // 2, q % 2
                    dve.wait_ge(bias_done, q + 1)
                    cut = slice(512 * c, 512 * (c + 1))
                    dve.tensor_tensor(xs[:, t, cut], bank[4 + q][:, :], xs[:, t, cut], ALU.add).then_inc(put_added, 1)
                dve.wait_ge(put_added, 4)

            def select(r, e):
                for t in range(TT):
                    ins = dve.tensor_scalar(sel[:, t, :], slots_f[:, bass.ds(r * CAP, CAP)], rank[:, t, bass.ds(e, 1)],
                                            None, ALU.is_equal)
                    ins.then_inc(sel_ready, 1)

            def select_weighted(r, e):
                for t in range(TT):
                    twice = slots_f[:, bass.ds(r * CAP, CAP)].unsqueeze(1).to_broadcast([P, 2, CAP])
                    ins = dve.tensor_scalar(selW[:, t, :, :], twice, rank[:, t, bass.ds(e, 1)],
                                            comb[:, t, bass.ds(e, 1)], ALU.is_equal, ALU.mult)
                    ins.then_inc(selW_ready, 1)

            def pick_expert(e):
                dve.tensor_copy(pick_e[:, :], ident[:, bass.ds(e, 1)].to_broadcast([P, CAP])).then_inc(pick_ready, 1)

            def take_turned(k):
                dve.wait_ge(got_turned, k)
                weights = g_moe.rearrange("p (h q) -> p q h", h=2)
                for h in range(2):
                    dve.tensor_tensor(gotT[:, :, h, :],
                                      bank[3][:, :].rearrange("p (q h c) -> p q h c", q=4, h=2)[:, :, h, :],
                                      weights[:, :, h].unsqueeze(2).to_broadcast([P, 4, CAP]),
                                      ALU.mult).then_inc(gotT_ready, 1)

            def expert(r, m, mg, p):
                e, n = m * 2 + p, mg * 2 + p
                dve.wait_ge(w1_used[p][1], mg + 1)
                dve.tensor_scalar(gate, bank[0][:, :], LIMIT, None, ALU.min).then_inc(gate_ready, 1)
                dve.wait_ge(w1_used[p][3], mg + 1)
                dve.tensor_scalar(lin, bank[1][:, :], LIMIT, -LIMIT, ALU.min, ALU.max).then_inc(ffn_step, 1)
                dve.wait_ge(gate_ready, n + 1)
                dve.wait_ge(ffn_step, n * 2 + 1)
                dve.scalar_tensor_tensor(out=lin, in0=lin, scalar=1.0, in1=gate, op0=ALU.add,
                                         op1=ALU.mult).then_inc(ffn_step, 1)
                dve.wait_ge(ffn_step, n * 2 + 2)
                dve.wait_ge(sig_ready, n + 1)
                dve.tensor_tensor(act_out, lin, sig, ALU.mult).then_inc(act_ready, 1)
                pick_expert(e + 1)
                dve.wait_ge(gather_done, n + r + 2)
                select(r, e + 2)
                dve.wait_ge(selT_done, n + 1)
                select_weighted(r, e + 1)
                take_turned(n + r + 2)
                for q, b in enumerate(PUT_BANKS):
                    t, half = q // 2, q % 2
                    dst = xs[:, t, 512 * half:512 * (half + 1)]
                    dve.wait_ge(put_done, n * 4 + q + 1)
                    dve.tensor_tensor(dst, bank[b][:, :], dst, ALU.add).then_inc(put_added, 1)

            def experts(r, first=False):
                select(r, 0)
                select_weighted(r, 0)
                pick_expert(0)
                dve.wait_ge(gather_done, r * (NE + 1) + 1)
                select(r, 1)
                take_turned(r * (NE + 1) + 1)
                if first:
                    add_biases()
                with dve.Fori(0, NE // 2) as m:
                    for p in range(2):
                        expert(r, m, r * (NE // 2) + m, p)
                dve.wait_ge(sel_ready, (r + 1) * (2 * (NE + 2)))
                dve.wait_ge(selW_ready, (r + 1) * (2 * (NE + 1)))
                dve.wait_ge(pick_ready, (r + 1) * (NE + 1))
                dve.wait_ge(gotT_ready, (r + 1) * (2 * (NE + 1)))
                dve.wait_ge(put_added, (r + 1) * (4 * NE) + 4)
                dve.sem_inc(round_end, 1)

            for_rounds(dve, experts)
            dve.memset(negmax[:, :], 0.0).then_inc(moe_end, 1)
            dve.wait_ge(final_in, 16)
            for t in range(TT):
                dve.tensor_tensor(weighted[t], xs[:, t, :], gfin[:, :], ALU.mult).then_inc(final_scaled, 1)
            dve.wait_ge(final_std, 1)
            dve.reciprocal(rstd[:, :, 0:1], std[:, :, 0:1]).then_inc(final_rstd, 1)
            dve.wait_ge(final_rstd, 1)
            dve.wait_ge(final_scaled, 2)
            dve.tensor_scalar(tn[:, 0, :], weighted[0], rstd[:, 0, 0:1], None, ALU.mult).then_inc(final_ready[0], 1)

        @block.tensor
        def _(pe):
            mm = pe.matmul

            def claim(b, user):
                if turn(b, user) > 1:
                    pe.wait_ge(drained[b], turn(b, user) - 1)

            def turn_rows(src, user):
                for q in range(4):
                    claim(4 + q, (user, q))
                    for c in range(2):
                        for t in range(TT):
                            ins = pe.transpose(bank[4 + q][:, S * c + P * t:S * c + P * (t + 1)],
                                               src(t, 2 * q + c), ident[:, :])
                    ins.then_inc(filled[4 + q], 1)

            pe.wait_ge(consts, ALL_CONSTS)
            pe.wait_ge(rows_in, 80)
            pe.transpose(bank[7][:, 0:64], rows[:, :], ident[0:64, 0:64]).then_inc(filled[7], 1)
            pe.wait_ge(scaled, 2)
            turn_rows(lambda t, c: xn[:, t, P * c:P * (c + 1)], "x")
            def project(i):
                name, kind, j, half = SLOTS[i]
                pe.wait_ge(weights_split, i + 1)
                if i >= 4:
                    if SLOTS[i - 4][0] in ON_DVE:
                        pe.wait_ge(dve_drained, dve_drains(i - 4))
                    else:
                        pe.wait_ge(act_drained, act_drains(i - 4))
                if j == 0 and half == 0:
                    if name in ("mk", "b0"):
                        for q in range(4):
                            pe.wait_ge(drained[4 + q], turn(4 + q, ("mem" if name == "mk" else "ml_y", q)))
                    elif name in ("b1", "b2"):
                        pe.wait_ge(o_split, {"b1": 1, "b2": 2}[name])
                hi, lo = (o_hi, o_lo) if name in ("mk", "mv", "b0", "b1", "b2") else (h_hi, h_lo)
                o, wh, wl = bank[i % 4], w_hi[i % 2], w_lo[i % 2]
                for c in range(2):
                    tile = slice(P * c, P * (c + 1))
                    for k in range(KT):
                        if i == 0 and c == 0 and k % 2 == 0:
                            pe.wait_ge(drained[4 + k // 2], turn(4 + k // 2, ("x", k // 2)))
                        if i == FIRST["out"] and c == 0 and k % 2 == 0:
                            pe.wait_ge(o_split, 3 + k // 2)
                        if kind == "T":
                            passes = [(wh[:, k, tile], hi[:, k, :]), (wh[:, k, tile], lo[:, k, :]),
                                      (wl[:, k, tile], hi[:, k, :])]
                        else:
                            passes = [(hi[:, k, tile], wh[:, k, :]), (hi[:, k, tile], wl[:, k, :]),
                                      (lo[:, k, tile], wh[:, k, :])]
                        for n, (stationary, moving) in enumerate(passes):
                            ins = mm(o[:, S * c:S * (c + 1)], stationary, moving, start=(k == 0 and n == 0),
                                     stop=(k == KT - 1 and n == 2))
                ins.then_inc(proj_done, 1)

            def gate_tokens():
                pe.wait_ge(gatew_in, 48)
                claim(4, ("gtok", 0))
                for t in range(TT):
                    for k in range(KT):
                        for part_of_h in (h_hi, h_lo):
                            ins = mm(bank[4][:, 16 * t:16 * (t + 1)], part_of_h[:, k, P * t:P * (t + 1)].bitcast(F32),
                                     wg[:, k, :], start=(k == 0 and part_of_h is h_hi),
                                     stop=(k == KT - 1 and part_of_h is h_lo))
                ins.then_inc(filled[4], 1)

            def gates():
                claim(4, ("gates", 0))
                for t in range(TT):
                    pe.transpose(bank[4][0:12, P * t:P * (t + 1)], gtok[:, t, 0:12], ident[:, :])
                    ins = pe.transpose(bank[4][0:4, S + P * t:S + P * (t + 1)], gtok[:, t, 12:16], ident[:, :])
                ins.then_inc(filled[4], 1)

            def gate_columns():
                pe.wait_ge(drained[4], turn(4, ("gates", 0)))
                claim(5, ("gcol", 0))
                for w, row in enumerate((arow, mrow)):
                    for t in range(TT):
                        c = 8 * w + 4 * t
                        ins = pe.transpose(bank[5][:, c:c + 4], row[:, P * t:P * (t + 1)], ident[0:4, 0:4])
                ins.then_inc(filled[5], 1)

            def mem_turn():
                pe.wait_ge(scaled, 4)
                turn_rows(lambda t, c: xn[:, t, P * c:P * (c + 1)], "mem")

            def turn_out(q):
                b = OUT_BANKS[q]
                pe.wait_ge(dve_drained, dve_drains(FIRST["out"] + q))
                claim(b, ("moe", q))
                for c in range(2):
                    for t in range(TT):
                        ins = pe.transpose(bank[b][:, S * c + P * t:S * c + P * (t + 1)],
                                           xs[:, t, P * (2 * q + c):P * (2 * q + c + 1)], ident[:, :])
                ins.then_inc(filled[b], 1)

            def ml_scores(h):
                if h == 0:
                    pe.wait_ge(qk_ready, 4)
                claim(5, ("ml_m", h))
                mm(bank[5][:, 0:256], pick[0:4, h, :], mrun[:, :], start=True, stop=True)
                mm(bank[5][:, 256:384], pick[0:4, h, :], mrun[:, P:S], start=True, stop=True).then_inc(filled[5], 1)
                claim(4, ("ml_s", h))
                mm(bank[4][:, 0:256], qkT[:, ML_H + h, 0:P], qkT[:, h, :], start=True, stop=True)
                mm(bank[4][:, 256:384], qkT[:, ML_H + h, P:S], qkT[:, h, P:S], start=True, stop=True).then_inc(filled[4], 1)

            def ml_values(h):
                pe.wait_ge(drained[4], turn(4, ("ml_s", h)))
                if h == 0:
                    pe.wait_ge(act_drained, act_drains(FIRST["mlv"] + 3))
                claim(6, ("ml_n0", h))
                mm(bank[6][:, 0:ML_DV + 1], p_t[:, 0:P], mval[:, 0, h, :], start=True, stop=True).then_inc(filled[6], 1)
                claim(7, ("ml_n1", h))
                mm(bank[7][:, 0:ML_DV + 1], p_t[:, P:S], mval[:, 0, h, :], start=True, stop=False)
                mm(bank[7][:, 0:ML_DV + 1], p_t[:, S:384], mval[:, 1, h, :], start=False, stop=True).then_inc(filled[7], 1)

            def ml_turn():
                pe.wait_ge(ml_y, 8)
                turn_rows(lambda t, c: num[:, t, c // 2, P * (c % 2):P * (c % 2 + 1)], "ml_y")

            def fx_scores(h):
                if h == 0:
                    pe.wait_ge(act_drained, act_drains(FIRST["fxk"] + 3))
                claim(4, ("fx_s", h))
                mm(bank[4][:, 0:128], fxqT[:, h, 0:P], fxkT[:, h, 0:P], start=True, stop=False)
                mm(bank[4][:, 0:128], pick[:, 4 + h, :], cF[:, 0:P], start=False, stop=True)
                mm(bank[4][:, 128:384], fxqT[:, h, P:S], fxkT[:, h, :], start=True, stop=False)
                mm(bank[4][:, 128:384], pick[:, 4 + h, :], cF[:, :], start=False, stop=True).then_inc(filled[4], 1)

            def fx_turn(h):
                pe.wait_ge(prob_ready, 2 * h + 2)
                claim(5, ("fx_p", h))
                for q in range(3):
                    ins = pe.transpose(bank[5][:, P * q:P * (q + 1)], p_b[:, P * q:P * (q + 1)], ident[:, :])
                ins.then_inc(filled[5], 1)

            def fx_values(h):
                pe.wait_ge(drained[5], turn(5, ("fx_p", h)))
                if h == 0:
                    pe.wait_ge(act_drained, act_drains(FIRST["fxv"] + 3))
                claim(6, ("fx_o", h))
                mm(bank[6][:, 0:S], fxv[:, 0, P * h:P * (h + 1)], p_t[:, 0:S], start=True, stop=False)
                mm(bank[6][:, P:S], fxv[:, 1, P * h:P * (h + 1)], p_t[:, S:384], start=False, stop=True).then_inc(filled[6], 1)

            def ca_scores(h):
                if h == 0:
                    pe.wait_ge(act_drained, act_drains(FIRST["caq"] + 3))
                claim(4, ("ca_s", h))
                for t in range(TT):
                    for k in range(2):
                        ins = mm(bank[4][:, S * t:S * (t + 1)], caqT[:, 2 * h + k, P * t:P * (t + 1)],
                                 kmT[:, 2 * h + k, :], start=(k == 0), stop=(k == 1))
                ins.then_inc(filled[4], 1)

            def ca_turn(h):
                pe.wait_ge(prob_ready, 2 * (FX_H + h) + 2)
                claim(5, ("ca_p", h))
                for m in range(2):
                    for t in range(TT):
                        ins = pe.transpose(bank[5][:, S * m + P * t:S * m + P * (t + 1)],
                                           p_b[:, S * t + P * m:S * t + P * (m + 1)], ident[:, :])
                ins.then_inc(filled[5], 1)

            def ca_values(h):
                pe.wait_ge(drained[5], turn(5, ("ca_p", h)))
                claim(6, ("ca_o", h))
                for c in range(2):
                    for m in range(2):
                        col = 256 * h + P * c
                        ins = mm(bank[6][:, S * c:S * (c + 1)], vm[:, m, col:col + P], p_t[:, S * m:S * (m + 1)],
                                 start=(m == 0), stop=(m == 1))
                ins.then_inc(filled[6], 1)

            work = dict(gate_tokens=gate_tokens, gates=gates, gate_columns=gate_columns, mem_turn=mem_turn, ml_scores=ml_scores,
                        ml_values=ml_values, ml_turn=ml_turn, turn_out=turn_out, fx_scores=fx_scores, fx_turn=fx_turn,
                        fx_values=fx_values, ca_scores=ca_scores, ca_turn=ca_turn, ca_values=ca_values)
            for i in range(len(SLOTS)):
                project(i)
                for name, *arg in STAGES.get(i, []):
                    if name in work:
                        work[name](*arg)

            pe.wait_ge(router_in, 32)

            def score(t, k0, k1):
                for k in range(k0, k1):
                    ins = mm(bank[t][:, 0:NE], tT[:, k, P * t:P * (t + 1)], wr[:, k, :],
                             start=(k == 0), stop=(k == KT - 1))
                return ins

            for q in range(3):
                pe.wait_ge(drained[OUT_BANKS[q]], turn(OUT_BANKS[q], ("moe", q)))
                for t in range(TT):
                    score(t, 2 * q, 2 * q + 2)
                if q == 1:
                    turn_out(3)
            pe.wait_ge(drained[OUT_BANKS[3]], turn(OUT_BANKS[3], ("moe", 3)))
            for t in range(TT):
                score(t, 6, 8).then_inc(logits_done, 1)
            pe.wait_ge(mask_ready, 1)
            mm(bank[3][:, 128:160], before[:, :], mask[:, 0, :], start=True, stop=True)
            mm(bank[3][:, 160:192], ones[:, :], mask[:, 0, :], start=True, stop=False)
            mm(bank[3][:, 160:192], before[:, :], mask[:, 1, :], start=False, stop=True)
            mm(bank[3][:, 192:224], ones[:, :], mask[:, 0, :], start=True, stop=False)
            mm(bank[3][:, 192:224], ones[:, :], mask[:, 1, :], start=False, stop=True).then_inc(rank_done, 1)

            def both_halves(o, lhsT, low, high, start, stop):
                mm(o[0:CAP, :], lhsT, low, start=start, stop=stop)
                return mm(o[CAP:P, :], lhsT, high, start=start, stop=stop)

            def gather(k):
                pe.wait_ge(sel_ready, k)
                for t in range(TT):
                    ins = both_halves(bank[2], sel[:, t, :], tn[:, t, 0:512], tn[:, t, 512:D], t == 0, t == TT - 1)
                ins.then_inc(gather_done, 1)

            def turn_gathered(k):
                pe.wait_ge(got_ready, k)
                for q in range(4):
                    ins = pe.transpose(bank[3][:, P * q:P * (q + 1)], got[:, P * q:P * (q + 1)], ident[:, :])
                ins.then_inc(got_turned, 1)

            pe.wait_ge(b1_in, 16)
            pe.wait_ge(scaled, 5)
            pe.wait_ge(scaled_act, 1)

            def expert(r, mg, p):
                n = mg * 2 + p
                pe.wait_ge(pick_ready, n + r + 1)
                pe.wait_ge(gotT_ready, n * 2 + r * 2 + 2)
                for part_ in range(2):
                    o, c = bank[part_], FF * part_
                    both_halves(o, pick_e[:, :], b1rows[:, c:c + 512], b1rows[:, c + 512:c + FF], True, False)
                    for k_half in range(2):
                        j = 2 * part_ + k_half
                        pe.wait_ge(w1_in[p][j], mg * 16 + 16)
                        for k in range(4):
                            w = w1_buf[p][j][:, k, :]
                            ins = both_halves(o, gotT[:, k, k_half, :], w[:, 0:512], w[:, 512:FF], False,
                                              k_half == 1 and k == 3)
                        ins.then_inc(w1_used[p][j], 1)
                pe.wait_ge(selW_ready, n * 2 + r * 2 + 2)
                pe.wait_ge(put_added, n * 4 + 4)
                gather(n * 2 + r * 4 + 4)
                for t in range(TT):
                    ins = pe.transpose(bank[6][:, P * t:P * (t + 1)],
                                       selW[:, t, :, :].rearrange("p o c -> p (o c)"), ident[:, :])
                ins.then_inc(selT_done, 1)
                pe.wait_ge(act_ready, n + 1)
                for q in range(4):
                    ins = pe.transpose(bank[4][:, P * q:P * (q + 1)], act_out[:, P * q:P * (q + 1)], ident[:, :])
                ins.then_inc(act_turned, 1)
                pe.wait_ge(aT_ready, n + 1)
                for j in range(W2):
                    pe.wait_ge(w2_in[j], n * 16 + 16)
                    for k in range(4):
                        w = w2_buf[j][:, k, :]
                        ins = both_halves(bank[5], aT[:, k, j, :], w[:, 0:512], w[:, 512:D], j == 0 and k == 0,
                                          j == W2 - 1 and k == 3)
                    ins.then_inc(w2_used[j], 1)
                turn_gathered(n + r + 2)
                pe.wait_ge(selWT_ready, n + 1)
                pe.wait_ge(yS_ready, n + 1)
                for q, b in enumerate(PUT_BANKS):
                    t, half = q // 2, slice(CAP * (q % 2), CAP * (q % 2 + 1))
                    mm(bank[b][:, :], selWT[half, t, :], yS[half, :], start=True, stop=True).then_inc(put_done, 1)

            def turn_comb():
                for t in range(TT):
                    ins = pe.transpose(bank[7][0:NE, P * t:P * (t + 1)], comb[:, t, 0:NE], ident[:, :])
                ins.then_inc(comb_turned, 1)

            def biases():
                pe.wait_ge(combT_ready, 1)
                pe.wait_ge(b2_in, 16)
                for q in range(4):
                    t, c = q // 2, q % 2
                    mm(bank[4 + q][:, :], combT[:, P * t:P * (t + 1)], b2rows[:, 512 * c:512 * (c + 1)],
                       start=True, stop=True).then_inc(bias_done, 1)

            def experts(r, first=False):
                gather(r * (2 * (NE + 2)) + 2)
                if first:
                    turn_comb()
                turn_gathered(r * (NE + 1) + 1)
                if first:
                    biases()
                with pe.Fori(0, NE // 2) as m:
                    for p in range(2):
                        expert(r, r * (NE // 2) + m, p)
                pe.wait_ge(gotT_ready, (r + 1) * (2 * (NE + 1)))
                pe.wait_ge(put_added, (r + 1) * (4 * NE) + 4)

            for_rounds(pe, experts)


_INS = ["x", "mem", "norm_mix", "w_in", "b_ml_gates", "conv_ml", "ml_head_norm", "b_fx_gate", "norm_mem",
        "w_mem_kv", "w_branch", "w_out", "norm_moe", "w_router", "b_router", "w_exp_in", "b_exp_in",
        "w_exp_out", "b_exp_out", "norm_final"]


def kernel(**inputs):
    import numpy as np
    import concourse.bacc as bacc
    from concourse.bass_utils import run_bass_kernel_spmd

    nc = bacc.Bacc("TRN2", target_bir_lowering=False, num_devices=1, dynamic_dma_scratch_size=1024)
    arrays, args = {}, []
    for name in _INS:
        a = np.ascontiguousarray(inputs[name])
        arrays[f"in_{name}"] = a
        args.append(nc.dram_tensor(f"in_{name}", a.shape, mybir.dt.from_np(a.dtype), kind="ExternalInput").ap())
    args.append(nc.dram_tensor("out_x", (1, S, D), F32, kind="ExternalOutput").ap())
    build(nc, *args)
    r = run_bass_kernel_spmd(nc, [arrays], core_ids=[0])
    return r.results[0]["out_x"]
```
